# Optimizing a Trainium2 kernel written in Bass

```python
import math
import jax, jax.numpy as jnp
from jax import lax
import numpy as np

D_MODEL = 1024
BATCH = 1
SEQ = 256
DEPTH = 1

D_MIX = D_MODEL
ATTN_HEADS = 8
ATTN_HD = 64
ATTN_W = ATTN_HEADS * ATTN_HD
MOBA_BLOCK = 256
MOBA_TOPK = 3
Q_BLOCK = 128
REC_HEADS = 4
REC_DK = 128
REC_DV = 128
REC_W = REC_HEADS * REC_DK
REC_VW = REC_HEADS * REC_DV
REC_CHUNK = 64
PEER_HEADS = 8
PEER_NKEYS = 128
PEER_N = PEER_NKEYS * PEER_NKEYS
PEER_DKEY = 256
PEER_TOPK = 16
PEER_TOKEN_BLOCK = 128
NORM_EPS = 1e-6
IN_WIDTHS = [ATTN_W, ATTN_W, ATTN_W, REC_W, REC_W, REC_VW, REC_VW]
IN_COLS = sum(IN_WIDTHS)
IN_SPLITS = [int(c) for c in np.cumsum(IN_WIDTHS)[:-1]]


def rmsnorm(x, g):
    xf = x.astype(jnp.float32)
    y = xf * lax.rsqrt(jnp.mean(xf * xf, axis=-1, keepdims=True) + NORM_EPS)
    return (y * g.astype(jnp.float32)).astype(x.dtype)

def alibi_slopes(n):
    return 2.0 ** (-8.0 * jnp.arange(1, n + 1, dtype=jnp.float32) / n)

def moba_attention(q, k, v):
    B, S, H, hd = q.shape
    nb = -(-S // MOBA_BLOCK)
    pad = nb * MOBA_BLOCK - S
    kp = jnp.pad(k, ((0, 0), (0, pad), (0, 0), (0, 0)))
    vp = jnp.pad(v, ((0, 0), (0, pad), (0, 0), (0, 0)))
    kb = kp.reshape(B, nb, MOBA_BLOCK, H, hd).transpose(0, 3, 1, 2, 4)
    vb = vp.reshape(B, nb, MOBA_BLOCK, H, hd).transpose(0, 3, 1, 2, 4)
    kmean = jnp.mean(kb.astype(jnp.float32), axis=3)
    gate = jnp.einsum('bshd,bhnd->bhsn', q.astype(jnp.float32), kmean)
    pos = jnp.arange(S)
    past = jnp.arange(nb)[None, :] < (pos // MOBA_BLOCK)[:, None]
    gate = jnp.where(past[None, None], gate, -jnp.inf)
    ksel = min(MOBA_TOPK, nb)
    _, sel = lax.top_k(gate, ksel)
    nq = S // Q_BLOCK
    qq = q.reshape(B, nq, Q_BLOCK, H, hd).transpose(0, 1, 3, 2, 4).reshape(B * nq, H, Q_BLOCK, hd)
    ss = sel.reshape(B, H, nq, Q_BLOCK, ksel).transpose(0, 2, 1, 3, 4).reshape(B * nq, H, Q_BLOCK, ksel)
    b_idx = jnp.repeat(jnp.arange(B, dtype=jnp.int32), nq)
    qb_idx = jnp.tile(jnp.arange(nq, dtype=jnp.int32), B)
    slopes = alibi_slopes(H)
    scale = hd ** -0.5
    off = jnp.arange(MOBA_BLOCK)
    gather = jax.vmap(lambda kk, s: kk[s])

    def one_block(args):
        qblk, sblk, b, qi = args
        kh = kb[b]
        vh = vb[b]
        tpos = qi * Q_BLOCK + jnp.arange(Q_BLOCK)
        own = (qi * Q_BLOCK) // MOBA_BLOCK
        k_s = gather(kh, sblk).astype(jnp.float32)
        v_s = gather(vh, sblk).astype(jnp.float32)
        k_o = lax.dynamic_index_in_dim(kh, own, axis=1, keepdims=False).astype(jnp.float32)
        v_o = lax.dynamic_index_in_dim(vh, own, axis=1, keepdims=False).astype(jnp.float32)
        qf = qblk.astype(jnp.float32) * scale
        s_sel = jnp.einsum('hqd,hqjkd->hqjk', qf, k_s)
        kpos_sel = sblk[..., None] * MOBA_BLOCK + off
        dist_sel = (tpos[None, :, None, None] - kpos_sel).astype(jnp.float32)
        s_sel = s_sel - slopes[:, None, None, None] * dist_sel
        s_sel = jnp.where((sblk < own)[..., None], s_sel, -jnp.inf)
        s_own = jnp.einsum('hqd,hkd->hqk', qf, k_o)
        kpos_own = own * MOBA_BLOCK + off
        dist_own = (tpos[:, None] - kpos_own[None, :]).astype(jnp.float32)
        s_own = s_own - slopes[:, None, None] * dist_own[None]
        s_own = jnp.where((kpos_own[None, :] <= tpos[:, None])[None], s_own, -jnp.inf)
        logits = jnp.concatenate([s_sel.reshape(H, Q_BLOCK, ksel * MOBA_BLOCK), s_own], axis=-1)
        p = jax.nn.softmax(logits, axis=-1)
        p_sel = p[..., :ksel * MOBA_BLOCK].reshape(H, Q_BLOCK, ksel, MOBA_BLOCK)
        p_own = p[..., ksel * MOBA_BLOCK:]
        o = jnp.einsum('hqjk,hqjkd->qhd', p_sel, v_s) + jnp.einsum('hqk,hkd->qhd', p_own, v_o)
        return o.astype(q.dtype)

    out = lax.map(one_block, (qq, ss, b_idx, qb_idx))
    return out.reshape(B, S, H * hd)

def hgrn2(q, f_pre, i, g, lb, norm_g):
    B, S, _ = q.shape
    nc = S // REC_CHUNK
    f = lb + (1.0 - lb) * jax.nn.sigmoid(f_pre.astype(jnp.float32))
    logf = jnp.log(f)
    kk = 1.0 - f
    qf = jax.nn.silu(q.astype(jnp.float32))
    vf = i.astype(jnp.float32)

    def heads(t, d):
        return t.reshape(B, nc, REC_CHUNK, REC_HEADS, d).transpose(1, 0, 3, 2, 4)

    causal = jnp.tril(jnp.ones((REC_CHUNK, REC_CHUNK), dtype=bool))

    def step(state, inp):
        qc, lfc, kc, vc = inp
        cum = jnp.cumsum(lfc, axis=2)
        diff = cum[:, :, :, None, :] - cum[:, :, None, :, :]
        decay = jnp.where(causal[None, None, :, :, None], jnp.exp(jnp.minimum(diff, 0.0)), 0.0)
        scores = jnp.einsum('bhtd,bhtsd,bhsd->bhts', qc, decay, kc)
        o = jnp.einsum('bhts,bhsv->bhtv', scores, vc) + jnp.einsum('bhtd,bhdv->bhtv', qc * jnp.exp(cum), state)
        last = cum[:, :, -1:, :]
        state = jnp.exp(last[:, :, 0, :])[..., None] * state + jnp.einsum('bhsd,bhsv->bhdv', kc * jnp.exp(last - cum), vc)
        return state, o

    state0 = jnp.zeros((B, REC_HEADS, REC_DK, REC_DV), jnp.float32)
    _, o = lax.scan(step, state0, (heads(qf, REC_DK), heads(logf, REC_DK), heads(kk, REC_DK), heads(vf, REC_DV)))
    o = o.transpose(1, 0, 3, 2, 4).reshape(B, S, REC_HEADS, REC_DV)
    o = rmsnorm(o, norm_g.reshape(REC_HEADS, REC_DV))
    o = o * jax.nn.silu(g.astype(jnp.float32)).reshape(B, S, REC_HEADS, REC_DV)
    return o.reshape(B, S, REC_VW).astype(q.dtype)

def peer(x, wq, subkeys, u, v):
    B, S, D = x.shape
    T = B * S
    xt = x.reshape(T // PEER_TOKEN_BLOCK, PEER_TOKEN_BLOCK, D)

    def one(xb):
        qp = (xb @ wq).reshape(PEER_TOKEN_BLOCK, PEER_HEADS, 2, PEER_DKEY // 2)
        s = jnp.einsum('thcd,hcnd->thcn', qp.astype(jnp.float32), subkeys.astype(jnp.float32))
        v1, i1 = lax.top_k(s[:, :, 0], PEER_TOPK)
        v2, i2 = lax.top_k(s[:, :, 1], PEER_TOPK)
        cand = (v1[..., :, None] + v2[..., None, :]).reshape(PEER_TOKEN_BLOCK, PEER_HEADS, PEER_TOPK * PEER_TOPK)
        cidx = (i1[..., :, None] * PEER_NKEYS + i2[..., None, :]).reshape(PEER_TOKEN_BLOCK, PEER_HEADS, PEER_TOPK * PEER_TOPK)
        sc, p = lax.top_k(cand, PEER_TOPK)
        eidx = jnp.take_along_axis(cidx, p, axis=-1)
        gates = jax.nn.softmax(sc, axis=-1)
        ue = u[eidx]
        ve = v[eidx]
        act = jax.nn.gelu(jnp.einsum('td,thkd->thk', xb, ue).astype(jnp.float32), approximate=False)
        return jnp.einsum('thk,thkd->td', (gates * act).astype(x.dtype), ve)

    return lax.map(one, xt).reshape(B, S, D)

def first_inputs(seed: int = 0) -> dict:
    key = jax.random.key(seed)
    ks = jax.random.split(key, 12)
    nrm = jax.random.normal
    x = nrm(ks[0], (BATCH, SEQ, D_MODEL), jnp.float32)
    norm1_g = 1.0 + 0.05 * nrm(ks[1], (DEPTH, D_MODEL), jnp.float32)
    w_in = nrm(ks[2], (DEPTH, D_MODEL, IN_COLS), jnp.float32) * D_MODEL ** -0.5
    rec_lb_logits = 0.5 * nrm(ks[3], (DEPTH + 1, REC_W), jnp.float32)
    rec_norm_g = 1.0 + 0.05 * nrm(ks[4], (DEPTH, REC_VW), jnp.float32)
    w_out = nrm(ks[5], (DEPTH, D_MIX, D_MODEL), jnp.float32) * D_MIX ** -0.5
    norm2_g = 1.0 + 0.05 * nrm(ks[6], (DEPTH, D_MODEL), jnp.float32)
    peer_wq = nrm(ks[7], (DEPTH, D_MODEL, PEER_HEADS * PEER_DKEY), jnp.float32) * D_MODEL ** -0.5
    peer_subkeys = nrm(ks[8], (DEPTH, PEER_HEADS, 2, PEER_NKEYS, PEER_DKEY // 2), jnp.float32) * (PEER_DKEY // 2) ** -0.5
    peer_u = nrm(ks[9], (DEPTH, PEER_N, D_MODEL), jnp.float32) * D_MODEL ** -0.5
    peer_v = 0.1 * nrm(ks[10], (DEPTH, PEER_N, D_MODEL), jnp.float32)
    normf_g = 1.0 + 0.05 * nrm(ks[11], (D_MODEL,), jnp.float32)
    return {'x': x, 'norm1_g': norm1_g, 'w_in': w_in, 'rec_lb_logits': rec_lb_logits,
            'rec_norm_g': rec_norm_g, 'w_out': w_out, 'norm2_g': norm2_g, 'peer_wq': peer_wq,
            'peer_subkeys': peer_subkeys, 'peer_u': peer_u, 'peer_v': peer_v, 'normf_g': normf_g}

def first_block(x, norm1_g, w_in, rec_lb_logits, rec_norm_g, w_out, norm2_g, peer_wq, peer_subkeys, peer_u, peer_v, normf_g):
    B, S, _ = x.shape
    lb_all = jnp.cumsum(jax.nn.softmax(rec_lb_logits.astype(jnp.float32), axis=0), axis=0)
    h = x
    for layer in range(DEPTH):
        xn = rmsnorm(h, norm1_g[layer])
        proj = xn @ w_in[layer]
        q_a, k_a, v_a, q_r, f_r, i_r, g_r = jnp.split(proj, IN_SPLITS, axis=-1)
        attn = moba_attention(q_a.reshape(B, S, ATTN_HEADS, ATTN_HD),
                              k_a.reshape(B, S, ATTN_HEADS, ATTN_HD),
                              v_a.reshape(B, S, ATTN_HEADS, ATTN_HD))
        rec = hgrn2(q_r, f_r, i_r, g_r, lb_all[layer], rec_norm_g[layer])
        h = h + jnp.concatenate([attn, rec], axis=-1) @ w_out[layer]
        hn = rmsnorm(h, norm2_g[layer])
        h = h + peer(hn, peer_wq[layer], peer_subkeys[layer], peer_u[layer], peer_v[layer])
    return rmsnorm(h, normf_g)


DEPTH_2 = 2

CHUNK = 64
HEAD_DIM = 64
CONV_WIDTH = D_MODEL // 2
LRU_WIDTH = D_MODEL // 2
CONV_GROUPS = CONV_WIDTH // HEAD_DIM
LRU_HEADS = LRU_WIDTH // HEAD_DIM
SHORT_CONV_K = 3
LRU_CONV_K = 4
RG_C = 8.0
SB_HEADS = D_MODEL // HEAD_DIM
D_FF = ((8 * D_MODEL // 3 + 255) // 256) * 256
N_MOD = 6
EPS = 1e-6


def rms_norm(x, g):
    x32 = x.astype(jnp.float32)
    y = x32 * lax.rsqrt(jnp.mean(x32 * x32, axis=-1, keepdims=True) + EPS)
    return (y * g.astype(jnp.float32)).astype(x.dtype)

def ada_modulation(c, ada_w, ada_b):
    m = jax.nn.silu(c) @ ada_w + ada_b
    return jnp.split(m, N_MOD, axis=-1)

def modulate(h, shift, scale):
    return h * (1.0 + scale[:, None, :]) + shift[:, None, :]

def causal_depthwise_conv(x, w):
    k_width = w.shape[0]
    seq = x.shape[1]
    xp = jnp.pad(x, ((0, 0), (k_width - 1, 0), (0, 0)))
    y = xp[:, 0:seq] * w[0]
    for k in range(1, k_width):
        y = y + xp[:, k:k + seq] * w[k]
    return y

def rg_lru(xr, w_a, b_a, w_x, b_x, lam):
    bsz, seq, width = xr.shape
    n_blk, blk = w_a.shape[0], w_a.shape[1]
    x32 = xr.astype(jnp.float32)
    xh = x32.reshape(bsz, seq, n_blk, blk)
    r = jax.nn.sigmoid(jnp.einsum('bshi,hij->bshj', xh, w_a.astype(jnp.float32)) + b_a).reshape(bsz, seq, width)
    i = jax.nn.sigmoid(jnp.einsum('bshi,hij->bshj', xh, w_x.astype(jnp.float32)) + b_x).reshape(bsz, seq, width)
    log_a = -RG_C * r * jax.nn.softplus(-lam.astype(jnp.float32))
    a = jnp.exp(log_a)
    b = jnp.sqrt(-jnp.expm1(2.0 * log_a)) * (i * x32)
    n_chunks = seq // CHUNK
    a_c = a.reshape(bsz, n_chunks, CHUNK, width).transpose(1, 0, 2, 3)
    b_c = b.reshape(bsz, n_chunks, CHUNK, width).transpose(1, 0, 2, 3)

    def combine(lhs, rhs):
        al, bl = lhs
        ar, br = rhs
        return al * ar, ar * bl + br

    def chunk_step(h0, ab):
        a_k, b_k = ab
        a_cum, b_cum = lax.associative_scan(combine, (a_k, b_k), axis=1)
        h = a_cum * h0[:, None, :] + b_cum
        return h[:, -1], h

    h_init = jnp.zeros((bsz, width), jnp.float32)
    _, hs = lax.scan(chunk_step, h_init, (a_c, b_c))
    return hs.transpose(1, 0, 2, 3).reshape(bsz, seq, width)

def stick_breaking_attention(q, k, v):
    seq, dh = q.shape[2], q.shape[3]
    scale = dh ** -0.5
    outs = []
    for blk in range(seq // Q_BLOCK):
        q0, q1 = blk * Q_BLOCK, (blk + 1) * Q_BLOCK
        qb = q[:, :, q0:q1].astype(jnp.float32)
        kb = k[:, :, :q1].astype(jnp.float32)
        vb = v[:, :, :q1].astype(jnp.float32)
        z = jnp.einsum('bhqd,bhkd->bhqk', qb, kb) * scale
        q_pos = jnp.arange(q0, q1)[:, None]
        k_pos = jnp.arange(q1)[None, :]
        strict = k_pos < q_pos
        log_keep = jnp.where(strict, jax.nn.log_sigmoid(-z), 0.0)
        prefix = jnp.cumsum(log_keep, axis=-1)
        after = prefix[..., -1:] - prefix
        w = jnp.where(strict, jnp.exp(jax.nn.log_sigmoid(z) + after), 0.0)
        outs.append(jnp.einsum('bhqk,bhkd->bhqd', w, vb))
    return jnp.concatenate(outs, axis=2)

def swiglu(h, w_gate, w_up, w_down):
    return (jax.nn.silu(h @ w_gate) * (h @ w_up)) @ w_down

def even_layer(x, c, ada_w, ada_b, mix_norm, w_in, conv_a_w, conv_b_w, conv_b_b,
               rg_a_w, rg_a_b, rg_x_w, rg_x_b, rg_lambda, w_out,
               ffn_norm, ffn_w_gate, ffn_w_up, ffn_w_down):
    sh_m, sc_m, g_m, sh_f, sc_f, g_f = ada_modulation(c, ada_w, ada_b)
    h = modulate(rms_norm(x, mix_norm), sh_m, sc_m)
    u = h @ w_in
    cuts = [CONV_WIDTH, 2 * CONV_WIDTH, 3 * CONV_WIDTH, 3 * CONV_WIDTH + LRU_WIDTH]
    a_b, a_c, a_x, r_gate, r_x = jnp.split(u, cuts, axis=-1)
    y_a = a_b * causal_depthwise_conv(a_c * a_x, conv_a_w)
    xr = causal_depthwise_conv(r_x, conv_b_w) + conv_b_b
    y_b = jax.nn.gelu(r_gate) * rg_lru(xr, rg_a_w, rg_a_b, rg_x_w, rg_x_b, rg_lambda).astype(x.dtype)
    y = jnp.concatenate([y_a, y_b], axis=-1) @ w_out
    x = x + g_m[:, None, :] * y
    hf = modulate(rms_norm(x, ffn_norm), sh_f, sc_f)
    return x + g_f[:, None, :] * swiglu(hf, ffn_w_gate, ffn_w_up, ffn_w_down)

def odd_layer(x, c, ada_w, ada_b, mix_norm, w_qkv, q_norm, k_norm, w_out,
              ffn_norm, ffn_w_gate, ffn_w_up, ffn_w_down):
    sh_m, sc_m, g_m, sh_f, sc_f, g_f = ada_modulation(c, ada_w, ada_b)
    h = modulate(rms_norm(x, mix_norm), sh_m, sc_m)
    bsz, seq, _ = x.shape
    qkv = (h @ w_qkv).reshape(bsz, seq, 3, SB_HEADS, HEAD_DIM)
    q = rms_norm(qkv[:, :, 0], q_norm).transpose(0, 2, 1, 3)
    k = rms_norm(qkv[:, :, 1], k_norm).transpose(0, 2, 1, 3)
    v = qkv[:, :, 2].transpose(0, 2, 1, 3)
    o = stick_breaking_attention(q, k, v).astype(x.dtype)
    o = o.transpose(0, 2, 1, 3).reshape(bsz, seq, SB_HEADS * HEAD_DIM)
    x = x + g_m[:, None, :] * (o @ w_out)
    hf = modulate(rms_norm(x, ffn_norm), sh_f, sc_f)
    return x + g_f[:, None, :] * swiglu(hf, ffn_w_gate, ffn_w_up, ffn_w_down)

def second_inputs(seed: int = 0) -> dict:
    key = jax.random.key(seed)
    ks = jax.random.split(key, 40)
    f32 = jnp.float32

    def nrm(k, shape, scale):
        return jax.random.normal(k, shape, f32) * scale

    d = D_MODEL
    u = jax.random.uniform(ks[12], (LRU_WIDTH,), f32, 0.9, 0.999)
    a0 = u ** (1.0 / RG_C)
    lam = jnp.log(a0) - jnp.log1p(-a0)
    return {
        'x': nrm(ks[0], (BATCH, SEQ, d), 1.0),
        'c': nrm(ks[1], (BATCH, d), 1.0),
        'l0_ada_w': nrm(ks[2], (d, N_MOD * d), 0.5 * d ** -0.5),
        'l0_ada_b': nrm(ks[3], (N_MOD * d,), 0.02),
        'l0_mix_norm': 1.0 + nrm(ks[4], (d,), 0.02),
        'l0_w_in': nrm(ks[5], (d, 3 * CONV_WIDTH + 2 * LRU_WIDTH), d ** -0.5),
        'l0_conv_a_w': nrm(ks[6], (SHORT_CONV_K, CONV_WIDTH), SHORT_CONV_K ** -0.5),
        'l0_conv_b_w': nrm(ks[7], (LRU_CONV_K, LRU_WIDTH), LRU_CONV_K ** -0.5),
        'l0_conv_b_b': nrm(ks[8], (LRU_WIDTH,), 0.01),
        'l0_rg_a_w': nrm(ks[9], (LRU_HEADS, HEAD_DIM, HEAD_DIM), HEAD_DIM ** -0.5),
        'l0_rg_a_b': nrm(ks[10], (LRU_HEADS, HEAD_DIM), 0.01),
        'l0_rg_x_w': nrm(ks[11], (LRU_HEADS, HEAD_DIM, HEAD_DIM), HEAD_DIM ** -0.5),
        'l0_rg_x_b': nrm(ks[13], (LRU_HEADS, HEAD_DIM), 0.01),
        'l0_rg_lambda': lam,
        'l0_w_out': nrm(ks[14], (CONV_WIDTH + LRU_WIDTH, d), (CONV_WIDTH + LRU_WIDTH) ** -0.5),
        'l0_ffn_norm': 1.0 + nrm(ks[15], (d,), 0.02),
        'l0_ffn_w_gate': nrm(ks[16], (d, D_FF), d ** -0.5),
        'l0_ffn_w_up': nrm(ks[17], (d, D_FF), d ** -0.5),
        'l0_ffn_w_down': nrm(ks[18], (D_FF, d), D_FF ** -0.5),
        'l1_ada_w': nrm(ks[19], (d, N_MOD * d), 0.5 * d ** -0.5),
        'l1_ada_b': nrm(ks[20], (N_MOD * d,), 0.02),
        'l1_mix_norm': 1.0 + nrm(ks[21], (d,), 0.02),
        'l1_w_qkv': nrm(ks[22], (d, 3 * SB_HEADS * HEAD_DIM), d ** -0.5),
        'l1_q_norm': 1.0 + nrm(ks[23], (HEAD_DIM,), 0.02),
        'l1_k_norm': 1.0 + nrm(ks[24], (HEAD_DIM,), 0.02),
        'l1_w_out': nrm(ks[25], (SB_HEADS * HEAD_DIM, d), (SB_HEADS * HEAD_DIM) ** -0.5),
        'l1_ffn_norm': 1.0 + nrm(ks[26], (d,), 0.02),
        'l1_ffn_w_gate': nrm(ks[27], (d, D_FF), d ** -0.5),
        'l1_ffn_w_up': nrm(ks[28], (d, D_FF), d ** -0.5),
        'l1_ffn_w_down': nrm(ks[29], (D_FF, d), D_FF ** -0.5),
    }

def second_block(x, c,
              l0_ada_w, l0_ada_b, l0_mix_norm, l0_w_in, l0_conv_a_w, l0_conv_b_w, l0_conv_b_b,
              l0_rg_a_w, l0_rg_a_b, l0_rg_x_w, l0_rg_x_b, l0_rg_lambda, l0_w_out,
              l0_ffn_norm, l0_ffn_w_gate, l0_ffn_w_up, l0_ffn_w_down,
              l1_ada_w, l1_ada_b, l1_mix_norm, l1_w_qkv, l1_q_norm, l1_k_norm, l1_w_out,
              l1_ffn_norm, l1_ffn_w_gate, l1_ffn_w_up, l1_ffn_w_down):
    even_params = [(l0_ada_w, l0_ada_b, l0_mix_norm, l0_w_in, l0_conv_a_w, l0_conv_b_w, l0_conv_b_b,
                    l0_rg_a_w, l0_rg_a_b, l0_rg_x_w, l0_rg_x_b, l0_rg_lambda, l0_w_out,
                    l0_ffn_norm, l0_ffn_w_gate, l0_ffn_w_up, l0_ffn_w_down)]
    odd_params = [(l1_ada_w, l1_ada_b, l1_mix_norm, l1_w_qkv, l1_q_norm, l1_k_norm, l1_w_out,
                   l1_ffn_norm, l1_ffn_w_gate, l1_ffn_w_up, l1_ffn_w_down)]
    for layer in range(DEPTH_2):
        if layer % 2 == 0:
            x = even_layer(x, c, *even_params[layer // 2])
        else:
            x = odd_layer(x, c, *odd_params[layer // 2])
    return x


def setup_inputs(seed=0):
    out = dict(first_inputs(seed))
    for name, value in second_inputs(seed + 1).items():
        if name != "x":
            out[name + "_2"] = value
    return out


def reference(
    x, norm1_g, w_in, rec_lb_logits, rec_norm_g, w_out, norm2_g, peer_wq, peer_subkeys, peer_u,
    peer_v, normf_g, c_2, l0_ada_w_2, l0_ada_b_2, l0_mix_norm_2, l0_w_in_2, l0_conv_a_w_2,
    l0_conv_b_w_2, l0_conv_b_b_2, l0_rg_a_w_2, l0_rg_a_b_2, l0_rg_x_w_2, l0_rg_x_b_2,
    l0_rg_lambda_2, l0_w_out_2, l0_ffn_norm_2, l0_ffn_w_gate_2, l0_ffn_w_up_2, l0_ffn_w_down_2,
    l1_ada_w_2, l1_ada_b_2, l1_mix_norm_2, l1_w_qkv_2, l1_q_norm_2, l1_k_norm_2, l1_w_out_2,
    l1_ffn_norm_2, l1_ffn_w_gate_2, l1_ffn_w_up_2, l1_ffn_w_down_2,
):
    x = first_block(
        x, norm1_g, w_in, rec_lb_logits, rec_norm_g, w_out, norm2_g, peer_wq, peer_subkeys,
        peer_u, peer_v, normf_g,
    )
    return second_block(
        x, c_2, l0_ada_w_2, l0_ada_b_2, l0_mix_norm_2, l0_w_in_2, l0_conv_a_w_2, l0_conv_b_w_2,
        l0_conv_b_b_2, l0_rg_a_w_2, l0_rg_a_b_2, l0_rg_x_w_2, l0_rg_x_b_2, l0_rg_lambda_2,
        l0_w_out_2, l0_ffn_norm_2, l0_ffn_w_gate_2, l0_ffn_w_up_2, l0_ffn_w_down_2, l1_ada_w_2,
        l1_ada_b_2, l1_mix_norm_2, l1_w_qkv_2, l1_q_norm_2, l1_k_norm_2, l1_w_out_2,
        l1_ffn_norm_2, l1_ffn_w_gate_2, l1_ffn_w_up_2, l1_ffn_w_down_2,
    )


_drawn_inputs = setup_inputs


def setup_inputs(seed=0):
    import zlib

    import numpy as np

    out = dict(_drawn_inputs(seed))
    spreads = {}
    factors = {'norm2_g': 4.53,
     'l0_mix_norm_2': 5.714,
     'l0_conv_b_b_2': 64.0,
     'l0_rg_a_b_2': 200.0,
     'l0_rg_x_b_2': 200.0,
     'l0_ffn_norm_2': 43.364,
     'l1_mix_norm_2': 200.0,
     'l1_q_norm_2': 200.0,
     'l1_k_norm_2': 200.0,
     'l1_ffn_norm_2': 53.483}
    for name, (base, spread) in spreads.items():
        noise = np.random.default_rng([zlib.crc32(name.encode()), seed]).standard_normal(out[name].shape)
        drawn = base * np.exp(spread * noise) if base else spread * noise
        out[name] = __import__('jax').numpy.asarray(drawn.astype(out[name].dtype))
    for name, factor in factors.items():
        out[name] = (out[name] * factor).astype(out[name].dtype)
    return out
```

```python
from contextlib import ExitStack

import numpy as np

import concourse.bass as bass
from concourse import mybir

F32 = mybir.dt.float32
I32 = mybir.dt.int32
U32 = mybir.dt.uint32
ALU = mybir.AluOpType
ACT = mybir.ActivationFunctionType
AX = mybir.AxisListType

P = 128
D = 1024
T = 256
KT = D // P
TT = T // P
HEADS, HD = 8, 64
RH = 4
PH, NK, TOPK = 8, 128, 16
SLOTS = PH * TOPK
FF = 2816
FU = FF // P
LH, LW = 4, 512
SBH = 16
EPS = 1e-6
NEG = -1e30

LAYERS = [("inproj", 14), ("outproj", 4), ("peerq", 8), ("ada", 32), ("l0in", 10), ("l0out", 4),
          ("ffn0", FU), ("qkv", 12), ("l1out", 4), ("ffn1", FU)]
UNIT0, UNITS = {}, {}
_at = 0
for _name, _n in LAYERS:
    UNIT0[_name], UNITS[_name] = _at, _n
    _at += _n
UNIT_COLS = {"ada": 3072, "ffn0": 3072, "ffn1": 3072}
RING = 4
RING_COLS = 3072
ADA_COLS = 384
GRING = 8
PRIME = 32

COLS = [("norm1", 8), ("norm2", 8), ("normf", 8), ("lb", 8), ("recg", 4), ("c", 8), ("adab", 96),
        ("mix0", 8), ("ffng0", 8), ("mix1", 8), ("ffng1", 8), ("wa", 12), ("wb", 16), ("bb", 4),
        ("ba", 4), ("bx", 4), ("lam", 4), ("qn", 1), ("kn", 1), ("one", 1), ("eps", 1)]
COL = {}
_at = 0
for _name, _n in COLS:
    COL[_name] = (_at, _n)
    _at += _n
NCOLS = _at
LEVELS = [128, 64, 32, 16, 8, 4, 2, 1]


def at_head(i, c):
    return 4 * (i // 2) + i % 2 + 2 * c if i < 4 else (i - 4) + 2 * c


def build(nc, xT, cols_d, w_d, alibi_d, masks_d, ident_d, tri_d, blk_d, sbmask_d, iota_d, subk_d, rg_d,
          u_d, v_d, out):
    with ExitStack() as ctx:
        def sb(name, shape, dt=F32):
            return ctx.enter_context(nc.sbuf_tensor(name, shape, dt))

        def sem(name):
            return ctx.enter_context(nc.semaphore(name))

        bank = [ctx.enter_context(nc.psum_tensor(f"bank{i}", [P, 512], F32)) for i in range(8)]
        NORM = bank[7]

        ring = sb("ring", [P, RING, RING_COLS])
        hT = sb("hT", [P, KT, T])
        xn = sb("xn", [P, KT, T])
        sq = sb("sq", [P, KT, T])
        rstd = sb("rstd", [P, T])
        lnv = sb("lnv", [P, T])
        cols = sb("cols", [P, NCOLS])
        ones = sb("ones", [P, P])
        ident = sb("ident", [P, P])
        mcol = sb("mcol", [P, 96])
        gain = sb("gain", [P, 4, 8])
        silc = sb("silc", [P, 8])
        small = sb("small", [P, 64])
        ARENA = 31500
        arena = sb("arena", [P, ARENA])
        S = {}

        def place(base, items):
            at = base
            for name, shape, *dt in items:
                n = int(np.prod(shape))
                v = arena[:, at:at + n]
                if dt:
                    v = v.bitcast(dt[0])
                if len(shape) == 2:
                    v = v.rearrange("p (a b) -> p a b", b=shape[1])
                elif len(shape) == 3:
                    v = v.rearrange("p (a b c) -> p a b c", b=shape[1], c=shape[2])
                S[name] = v
                at += n
            assert at <= ARENA, (at, items[0][0])
            return at

        place(0, [("qf", (4, 256)), ("fT", (4, 256)), ("lf", (4, 256)), ("kk", (4, 256)), ("cum", (4, 256)),
                  ("D0", (4, 256)), ("D1", (4, 256)), ("K0", (4, 256)), ("K1", (4, 256)),
                  ("Q0", (4, 256)), ("Q1", (4, 256)), ("irow", (2, 512)), ("grow", (2, 512)),
                  ("qa", (4, 256)), ("ka", (4, 256)), ("va", (2, 512)), ("STd", (4, 2, 128)), ("ST01", (4, 128)),
                  ("L0", (512,)), ("L1", (512,)), ("P0", (512,)), ("P1", (512,)), ("PT0", (4, 128)), ("PT1", (4, 128)),
                  ("alibi", (6, 512)), ("masks", (7, 128), I32), ("osq", (4, 128)), ("orow0", (4, 128)),
                  ("orow1", (4, 128)), ("osm", (64,)), ("cat", (8, 256))])
        place(0, [("qpT", (16, 256)), ("s", (16, 128)), ("s2", (16, 128)), ("hnrow", (2, 1024)),
                  ("v16", (16, 16)), ("i16", (16, 16), U32), ("if16", (16, 16)), ("cand", (8, 256)),
                  ("cand2", (8, 256)), ("sc", (8, 16)), ("pos", (8, 16), U32), ("posa", (128,), U32),
                  ("posb", (128,), U32), ("fa", (128,)), ("fb", (128,)), ("e1", (128,)),
                  ("e2", (128,)), ("idx", (2, 128), I32), ("gates", (2, 128)), ("act", (2, 128)),
                  ("gel", (128,)), ("wts", (2, 128)), ("rows", (GRING, 1024)), ("istage", (2, 16), I32), ("astage", (2, 16)), ("tiny", (64,)),
                  ("mrow", (2, 384)), ("subk", (16, 128)), ("iota", (16,))])
        S["acc"] = arena[:, 0:4096].rearrange("p (a b) -> p a b", b=1024)
        S["oh"] = arena[:, 6144:8192].rearrange("p (a b) -> p a b", b=16)
        S["junk"] = S["cand2"].rearrange("p a b -> p (a b)").rearrange("p (a b) -> p a b", b=1024)
        place(0, [("rxp", (4, 259)), ("gg", (4, 256)), ("ac", (4, 256)), ("prod", (4, 258)), ("xr", (4, 256)),
                  ("cv", (4, 256)), ("rT", (4, 256)), ("iT", (4, 256)), ("aT", (4, 256)), ("tT", (4, 256)),
                  ("l1", (4, 256)), ("l2", (4, 256)), ("bT", (4, 256)), ("hs", (4, 256)), ("ix", (4, 256)),
                  ("cat0", (8, 256)), ("rgw", (8, 128))])
        e = place(18000, [("sg0", (256,)), ("sg1", (256,)), ("fa0", (256,)), ("fa1", (256,))])
        place(0, [("qT", (8, 256)), ("kT", (8, 256)), ("vrow", (2, 1024)), ("sqh", (2, 512)), ("rsh", (2, 512)),
                  ("lnh", (512,))] +
              [(f"{n}{i}", (384,)) for n in ("az", "ez", "lz", "sp", "lk", "ls", "wz") for i in (0, 1)] +
              [("oT", (8, 256)), ("tri", (128,)), ("blk", (128,)), ("sbmask", (2, 384))])

        def col(name, i=0, n=1):
            return cols[:, COL[name][0] + i:COL[name][0] + i + n]

        x_in = sem("x_in")
        const_in = sem("const_in")
        peer_in = sem("peer_in")
        late_in = sem("late_in")
        landed = [sem(f"landed{i}") for i in range(RING)]
        unit_done = sem("unit_done")
        unit_out = [sem(f"unit_out{i}") for i in range(2)]
        ffn_used = sem("ffn_used")
        ffn_silu = sem("ffn_silu")
        norm_sq, norm_sum, norm_rs, norm_out, norm_mod = (sem(n) for n in (
            "norm_sq", "norm_sum", "norm_rs", "norm_out", "norm_mod"))
        h_new = sem("h_new")
        dve_seq, act_seq, pool_seq = sem("dve_seq"), sem("act_seq"), sem("pool_seq")
        hg_f, hg_lf, hg_kk, hg_cum, hg_d, hg_e, hg_kq, hg_ps, hg_st = (sem(n) for n in (
            "hg_f", "hg_lf", "hg_kk", "hg_cum", "hg_d", "hg_e", "hg_kq", "hg_ps", "hg_st"))
        rec_o, rec_ss, rec_var, rec_rs, rec_row, rec_t, rec_cat = (sem(n) for n in (
            "rec_o", "rec_ss", "rec_var", "rec_rs", "rec_row", "rec_t", "rec_cat"))
        at_s, at_l, at_mx, at_p, at_pn, at_t, at_pt, at_o, at_cat = (sem(n) for n in (
            "at_s", "at_l", "at_mx", "at_p", "at_pn", "at_t", "at_pt", "at_o", "at_cat"))
        hn_t, hn_row, sc_ps, sc_in, sc_used, idx_ready, sc_sub, gate_e, dots_kept, act_gelu, wts_ready, acc_ready, po_t = (
            sem(n) for n in ("hn_t", "hn_row", "sc_ps", "sc_in", "sc_used", "idx_ready", "sc_sub", "gate_e",
                             "dots_kept", "act_gelu", "wts_ready", "acc_ready", "po_t"))
        row_in = [sem(f"row_in{i}") for i in range(GRING)]
        rows_used = sem("rows_used")
        staged, waited = sem("staged"), sem("waited")
        silc_ready, mrow_ready, mcol_ps, mcol_ready, lam_a, lam_b = (sem(n) for n in (
            "silc_ready", "mrow_ready", "mcol_ps", "mcol_ready", "lam_a", "lam_b"))
        xr_ready, rg_ps, rg_sig, lru_t, lru_c, lru_l, lru_d, lru_s, lru_ix, cat0_ready, ac_ready = (sem(n) for n in (
            "xr_ready", "rg_ps", "rg_sig", "lru_t", "lru_c", "lru_l", "lru_d", "lru_s", "lru_ix", "cat0_ready",
            "ac_ready"))
        ffn_acc = sem("ffn_acc")
        qk_sq, qk_sum, qk_rs, qk_ready, z_ps, z_ln, z_sp, z_ls, z_lk, z_af, z_arg, z_w, z_wm, z_o, z_out = (sem(n) for n in (
            "qk_sq", "qk_sum", "qk_rs", "qk_ready", "z_ps", "z_ln", "z_sp", "z_ls", "z_lk", "z_af", "z_arg", "z_w", "z_wm",
            "z_o", "z_out"))
        stored = sem("stored")

        class Order:

            def __init__(self, eng, s):
                self.eng, self.s, self.n = eng, s, 0

            def mark(self, ins):
                ins.then_inc(self.s, 1)
                self.n += 1
                return self.n

            def wait(self, n=None):
                self.eng.wait_ge(self.s, self.n if n is None else n)

        H_MIX, H_PEER, H_F, H_L0, H_FFN0, H_L1, H_FINAL = 4, 8, 16, 24, 32, 40, 48

        def wait_unit_out(eng, g, it=0):
            for name, base, per in (("outproj", 0, 1), ("l0out", H_F, 2), ("l1out", H_FFN0, 2)):
                if UNIT0[name] <= g < UNIT0[name] + UNITS[name]:
                    eng.wait_ge(h_new, base + per * (g - UNIT0[name] + 1))
                    return
            joined = sum(1 for n in ("outproj", "l0out", "l1out") for j in range(UNITS[n])
                         if UNIT0[n] + j <= g and (UNIT0[n] + j) % 2 == g % 2)
            eng.wait_ge(unit_out[g % 2], it * 2 + (g // 2 + 1 - joined))

        def looped(eng, lo, hi, body):
            n = (hi - lo) // 4
            with eng.Fori(0, n) as it:
                for u in range(4):
                    body(it * 4 + (lo + u), lo + u, it)
            for j in range(lo + 4 * n, hi):
                body(j, j, 0)

        def flat(ap):
            return ap.rearrange("p a b -> p (a b)")


        block = ctx.enter_context(nc.Block())

        @block.sync
        def _(sp):
            def load(u, g, src, it=0):
                sp.dma_start(ring[:, g % RING, 0:src.shape[-1]], src).then_inc(landed[g % RING], 16)

            def wait_slot(g, it=0):
                b = g - RING
                if b < 0:
                    return
                for f, k in (("ffn0", 0), ("ffn1", 1)):
                    if UNIT0[f] <= b < UNIT0[f] + FU:
                        sp.wait_ge(ffn_used, it * 4 + (b - UNIT0[f] + 1 + FU * k))
                        return
                sp.wait_ge(unit_done, it * 4 + (b + 1))

            sp.dma_start(cols[:, :], cols_d).then_inc(x_in, 16)
            sp.dma_start(hT[:, :, :], xT).then_inc(x_in, 16)
            for j in range(UNITS["inproj"]):
                wait_slot(j)
                load(0, j, w_d["inproj"][j])
            for name in ("outproj", "peerq"):
                g0 = UNIT0[name]
                for j in range(UNITS[name]):
                    wait_slot(g0 + j)
                    load(0, g0 + j, w_d[name][j])
            for name in ("ada", "l0in", "l0out", "ffn0", "qkv", "l1out", "ffn1"):
                g0, n = UNIT0[name], UNITS[name]
                for j in range(4):
                    wait_slot(g0 + j)
                    load(0, g0 + j, w_d[name][j])

                def body(j, u, it):
                    wait_slot(g0 + u, it)
                    load(0, g0 + u, w_d[name][j])
                if n > 4:
                    looped(sp, 4, n, body)
            sp.wait_ge(h_new, H_FINAL)
            sp.dma_start(out, hT[:, :, :]).then_inc(stored, 16)
            sp.wait_ge(stored, 16)


        @block.gpsimd
        def _(pool):
            seq = Order(pool, pool_seq)
            g = nc.gpsimd
            g.memset(ones[:, :], 1.0).then_inc(x_in, 16)
            g.dma_start(ident[:, :], ident_d).then_inc(const_in, 16)
            g.dma_start(S["alibi"], alibi_d).then_inc(const_in, 16)
            g.dma_start(S["masks"], masks_d).then_inc(const_in, 16)
            for n in ("K0", "K1", "Q0", "Q1"):
                seq.mark(g.memset(flat(S[n]), 0.0))
            seq.wait()
            pool.wait_ge(hg_f, 4)
            g.tensor_scalar(flat(S["kk"]), flat(S["fT"]), -1.0, 1.0, ALU.mult, ALU.add).then_inc(hg_kk, 1)
            pool.wait_ge(hg_kk, 1)
            for i, b in enumerate(LEVELS):
                E = flat(S[f"D{i % 2}"]).rearrange("p (m two b) -> p m two b", two=2, b=b)
                kd = flat(S[f"K{i % 2}"]).rearrange("p (m two b) -> p m two b", two=2, b=b)
                qd = flat(S[f"Q{i % 2}"]).rearrange("p (m two b) -> p m two b", two=2, b=b)
                kk = flat(S["kk"]).rearrange("p (m two b) -> p m two b", two=2, b=b)
                qf = flat(S["qf"]).rearrange("p (m two b) -> p m two b", two=2, b=b)
                pool.wait_ge(hg_e, i + 1)
                if i == 0:
                    for g_ in (0, 1):
                        wait_unit_out(pool, g_)
                if i >= 2:
                    pool.wait_ge(hg_ps, i - 1)
                g.tensor_tensor(kd[:, :, 0, :], kk[:, :, 0, :], E[:, :, 0, :], ALU.mult).then_inc(hg_kq, 1)
                g.tensor_tensor(qd[:, :, 1, :], qf[:, :, 1, :], E[:, :, 1, :], ALU.mult).then_inc(hg_kq, 1)
            pool.wait_ge(h_new, H_MIX)
            g.dma_start(S["subk"], subk_d).then_inc(peer_in, 16)
            g.dma_start(S["iota"], iota_d).then_inc(peer_in, 16)

            for ph in range(4):
                tt, table = ph // 2, (u_d, v_d)[ph % 2]
                if ph % 2 == 0:
                    pool.wait_ge(idx_ready, tt + 1)
                n0 = ph * SLOTS
                with pool.Fori(0, SLOTS // 32) as it:
                    for hh in range(2):
                        pool.wait_ge(rows_used, it * 32 + (n0 + 16 * hh - 16 + PRIME))
                        pool.sem_inc(waited, 1)
                        g.tensor_copy(S["istage"][:, hh, :],
                                      S["idx"][:, tt, bass.ds(it * 32 + 16 * hh, 16)]).then_inc(staged, 1)
                        pool.wait_ge(staged, it * 2 + (ph * 8 + hh + 1))
                        pool.sem_inc(waited, 1)
                        for j in range(16):
                            n = n0 + 16 * hh + j
                            if j % 4 == 0:
                                pool.wait_ge(rows_used, it * 32 + (n + 4 - GRING + PRIME))
                                pool.sem_inc(waited, 1)
                            g.indirect_dma_start(S["rows"][:, n % GRING, :], None, table,
                                                 bass.IndirectOffsetOnAxis(S["istage"][:, hh, j:j + 1], 0)
                                                 ).then_inc(row_in[n % GRING], 16)
            pool.wait_ge(h_new, H_F)
            g.dma_start(S["rgw"], rg_d).then_inc(late_in, 16)
            seq.mark(g.memset(S["rxp"][:, :, 0:3], 0.0))
            seq.mark(g.memset(S["prod"][:, :, 0:2], 0.0))
            pool.wait_ge(rg_sig, 8)
            g.tensor_tensor(flat(S["ix"]), flat(S["iT"]), flat(S["xr"]), ALU.mult).then_inc(lru_ix, 1)
            pool.wait_ge(h_new, H_FFN0)
            g.dma_start(S["tri"], tri_d).then_inc(late_in, 16)
            g.dma_start(S["blk"], blk_d).then_inc(late_in, 16)
            g.dma_start(S["sbmask"], sbmask_d).then_inc(late_in, 16)
            pool.wait_ge(late_in, 64)
            for h in range(SBH):
                pool.wait_ge(z_w, h + 1)
                w = S[f"wz{h % 2}"].rearrange("p (c q) -> p c q", c=3)[:, 0:3:2, :]
                m = S["sbmask"][:, 1, :].rearrange("p (c q) -> p c q", c=3)[:, 0:3:2, :]
                g.tensor_tensor(w, w, m, ALU.mult).then_inc(z_wm, 1)

        @block.scalar
        def _(act):
            a = nc.scalar
            seq = Order(act, act_seq)

            def norm(n, need_h, modulated=None, shift=None):
                if need_h:
                    act.wait_ge(h_new, need_h)
                for k in range(KT):
                    a.activation(sq[:, k, :], hT[:, k, :], ACT.Square).then_inc(norm_sq, 1)
                act.wait_ge(norm_sum, n + 1)
                seq.mark(a.activation(lnv[:, :], NORM[:, 0:T], ACT.Ln, scale=1.0 / D, bias=col("eps")))
                seq.wait()
                a.activation(rstd[:, :], lnv[:, :], ACT.Exp, scale=-0.5).then_inc(norm_rs, 1)
                if shift is not None:
                    for k in range(KT):
                        act.wait_ge(norm_out, 8 * (n - 1) + k + 1)
                        a.activation(xn[:, k, :], xn[:, k, :], ACT.Identity, bias=shift[:, k:k + 1]
                                     ).then_inc(norm_mod, 1)

            def read_unit(g, fn, dst, **kw):
                act.wait_ge(unit_done, g + 1)
                a.activation(dst, bank[g % 2][:, :], fn, **kw).then_inc(unit_out[g % 2], 1)

            act.wait_ge(x_in, 48)
            norm(0, 0)
            read_unit(0, ACT.Silu, flat(S["qf"][:, 0:2, :]))
            read_unit(1, ACT.Silu, flat(S["qf"][:, 2:4, :]))
            read_unit(2, ACT.Sigmoid, flat(S["fT"][:, 0:2, :]))
            read_unit(3, ACT.Sigmoid, flat(S["fT"][:, 2:4, :]))
            act.wait_ge(lam_a, 1)
            a.activation(small[:, 8:12], small[:, 4:8], ACT.Sigmoid).then_inc(lam_b, 1)
            act.wait_ge(hg_f, 4)
            a.activation(flat(S["lf"]), flat(S["fT"]), ACT.Ln).then_inc(hg_lf, 1)

            def level_exp(i):
                act.wait_ge(hg_d, 2 * i + 2)
                a.activation(flat(S[f"D{i % 2}"]), flat(S[f"D{i % 2}"]), ACT.Exp).then_inc(hg_e, 1)

            def at_exp(i):
                nh = 2 if i < 4 else 4
                w = 512 // nh
                act.wait_ge(at_mx, i + 1)
                for h in range(nh):
                    a.activation(S[f"P{i % 2}"][:, h * w:(h + 1) * w], S[f"L{i % 2}"][:, h * w:(h + 1) * w],
                                 ACT.Exp, bias=S["osm"][:, 8 * (i % 2) + h:8 * (i % 2) + h + 1],
                                 accum_out=S["osm"][:, 16 + 8 * (i % 2) + h:17 + 8 * (i % 2) + h]).then_inc(at_p, 1)

            def at_copy(i):
                act.wait_ge(at_t, i + 1)
                if i >= 2:
                    act.wait_ge(at_o, i - 1)
                a.activation(flat(S[f"PT{i % 2}"]), bank[5][:, :], ACT.Copy).then_inc(at_pt, 1)

            for u in range(4, 14):
                if u in (4, 5):
                    read_unit(u, ACT.Copy, flat(S["qa"][:, 2 * (u - 4):2 * (u - 4) + 2, :]), scale=HD ** -0.5)
                if u in (12, 13):
                    c = u - 12
                    read_unit(u, ACT.Silu, S["grow"][:, :, 256 * c:256 * c + 256])
                i = u - 4
                if i < 8:
                    level_exp(i)
                if 0 <= u - 9 < 6:
                    at_exp(u - 9)
                if 0 <= u - 10 < 6:
                    at_copy(u - 10)
            at_exp(5)
            at_copy(4)
            at_copy(5)
            for tt in range(TT):
                act.wait_ge(rec_o, tt + 1)
                if tt:
                    act.wait_ge(rec_var, 1)
                a.activation(flat(S["osq"]), bank[2 + tt][:, :], ACT.Square).then_inc(rec_ss, 1)
            act.wait_ge(rec_var, 2)
            seq.mark(a.activation(S["osm"][:, 40:48], S["osm"][:, 32:40], ACT.Ln, scale=1.0 / P, bias=col("eps")))
            seq.wait()
            a.activation(S["osm"][:, 48:56], S["osm"][:, 40:48], ACT.Exp, scale=-0.5).then_inc(rec_rs, 1)
            for tt in range(TT):
                act.wait_ge(rec_t, tt + 1)
                for h in range(RH):
                    a.activation(S["cat"][:, 4 + h, tt * P:(tt + 1) * P], bank[4 + tt][:, h * P:(h + 1) * P],
                                 ACT.Copy, scale=col("recg", h)).then_inc(rec_cat, 1)
            norm(1, H_MIX)
            for j in range(8):
                read_unit(UNIT0["peerq"] + j, ACT.Copy, flat(S["qpT"][:, 2 * j:2 * j + 2, :]))
            for q in range(8):
                act.wait_ge(sc_ps, q + 1)
                if q == 4:
                    act.wait_ge(sc_used, 1)
                a.activation(flat(S["s"][:, 4 * (q % 4):4 * (q % 4) + 4, :]), bank[[4, 5, 2, 3][q % 4]][:, :],
                             ACT.Copy).then_inc(sc_in, 1)
            for tt in range(TT):
                act.wait_ge(sc_sub, tt + 1)
                a.activation(S["gates"][:, tt, :], S["gates"][:, tt, :], ACT.Exp).then_inc(gate_e, 1)
            act.wait_ge(lam_a, 2)
            seq.mark(a.activation(small[:, 24:28], small[:, 20:24], ACT.Exp, scale=-1.0))
            seq.wait()
            a.activation(small[:, 28:32], small[:, 24:28], ACT.Ln, bias=col("one")).then_inc(lam_b, 1)
            a.activation(silc[:, :], col("c", 0, 8), ACT.Silu).then_inc(silc_ready, 1)
            G0 = UNIT0["ada"]

            def ada_row(j, u, it):
                act.wait_ge(unit_done, it * 4 + (G0 + u + 1))
                if not isinstance(j, int) or j >= 2:
                    act.wait_ge(mcol_ps, it * 4 + (u - 1))
                a.activation(S["mrow"][0:1, u % 2, :], bank[(G0 + u) % 2][0:1, 0:ADA_COLS], ACT.Copy
                             ).then_inc(unit_out[(G0 + u) % 2], 1)
            ada_row(0, 0, 0)
            ada_row(1, 1, 0)
            looped(act, 2, 32, ada_row)
            for tt in range(TT):
                act.wait_ge(dots_kept, 8 * (tt + 1))
                if tt:
                    act.wait_ge(wts_ready, 1)
                a.activation(S["gel"], S["act"][:, tt, :], ACT.Gelu).then_inc(act_gelu, 1)
            norm(2, H_PEER)
            norm(3, H_F, shift=mcol[:, 0:8])
            G0 = UNIT0["l0in"]
            act.wait_ge(h_new, H_F)
            for j in range(2):
                act.wait_ge(unit_done, G0 + j + 1)
                a.activation(S["rxp"][:, 2 * j:2 * j + 2, 3:259],
                             bank[(G0 + j) % 2][:, :].rearrange("p (a t) -> p a t", a=2), ACT.Copy
                             ).then_inc(unit_out[(G0 + j) % 2], 1)
            for j in (2, 3):
                read_unit(G0 + j, ACT.Gelu_apprx_tanh, flat(S["gg"][:, 2 * (j - 2):2 * (j - 2) + 2, :]))
            for j in (4, 5):
                read_unit(G0 + j, ACT.Copy, flat(S["ac"][:, 2 * (j - 4):2 * (j - 4) + 2, :]))
            for b in range(8):
                act.wait_ge(rg_ps, b // 2 + 1)
                dst = S["rT"] if b < 4 else S["iT"]
                a.activation(dst[:, b % 4, :], bank[2 + b // 2][:, 256 * (b % 2):256 * (b % 2) + 256], ACT.Sigmoid,
                             bias=col("ba" if b < 4 else "bx", b % 4)).then_inc(rg_sig, 1)
            act.wait_ge(rg_sig, 4)
            for b in range(LH):
                a.activation(S["aT"][:, b, :], S["rT"][:, b, :], ACT.Exp, scale=small[:, 36 + b:37 + b]
                             ).then_inc(lru_t, 1)
            for b in range(LH):
                a.activation(S["tT"][:, b, :], S["rT"][:, b, :], ACT.Tanh, scale=small[:, 32 + b:33 + b]
                             ).then_inc(lru_t, 1)
            act.wait_ge(lru_c, 1)
            a.activation(flat(S["l1"]), flat(S["tT"]), ACT.Ln, scale=2.0).then_inc(lru_l, 1)
            a.activation(flat(S["l2"]), flat(S["tT"]), ACT.Ln, bias=col("one")).then_inc(lru_l, 1)
            act.wait_ge(lru_d, 1)
            a.activation(flat(S["l1"]), flat(S["l1"]), ACT.Exp, scale=0.5).then_inc(lru_s, 1)
            norm(4, H_L0, shift=mcol[:, 24:32])

            def silu(f):
                G0 = UNIT0[f"ffn{f}"]

                def body(j, u, it):
                    act.wait_ge(unit_done, it * 4 + (G0 + u + 1))
                    a.activation(S[f"sg{u % 2}"], bank[(G0 + u) % 2][:, 0:256], ACT.Silu).then_inc(ffn_silu, 1)
                looped(act, 0, FU, body)
            silu(0)
            norm(5, H_FFN0, shift=mcol[:, 48:56])
            G0 = UNIT0["qkv"]

            def qk_rstd(i):
                act.wait_ge(qk_sum, i + 1)
                if i:
                    act.wait_ge(qk_rs, i)
                seq.mark(a.activation(S["lnh"], bank[2 + i % 2][:, :], ACT.Ln, scale=1.0 / HD, bias=col("eps")))
                seq.wait()
                if i >= 2:
                    act.wait_ge(qk_ready, i - 1)
                a.activation(S["rsh"][:, i % 2, :], S["lnh"], ACT.Exp, scale=-0.5).then_inc(qk_rs, 1)
            for i in range(8):
                dst = flat((S["qT"] if i < 4 else S["kT"])[:, 2 * (i % 4):2 * (i % 4) + 2, :])
                read_unit(G0 + i, ACT.Copy, dst)
                wait_unit_out(act, G0 + i)
                if i >= 2:
                    act.wait_ge(qk_sum, i - 1)
                a.activation(S["sqh"][:, i % 2, :], dst, ACT.Square).then_inc(qk_sq, 1)
                if i:
                    qk_rstd(i - 1)
            qk_rstd(7)
            for c in range(4):
                read_unit(G0 + 8 + c, ACT.Copy, S["vrow"][:, :, 256 * c:256 * c + 256])

            def z_first(h):
                act.wait_ge(z_ps, h + 1)
                b = h % 2
                seq.mark(a.activation(S[f"az{b}"], bank[2 + b][:, 0:384], ACT.Abs))
                seq.wait()
                seq.mark(a.activation(S[f"ez{b}"], S[f"az{b}"], ACT.Exp, scale=-1.0))
                seq.wait()
                if h >= 2:
                    act.wait_ge(z_sp, h - 1)
                a.activation(S[f"lz{b}"], S[f"ez{b}"], ACT.Ln, bias=col("one")).then_inc(z_ln, 1)

            def z_second(h):
                act.wait_ge(z_arg, h + 1)
                if h >= 2:
                    act.wait_ge(z_o, h - 1)
                a.activation(S[f"wz{h % 2}"], S[f"ls{h % 2}"], ACT.Exp).then_inc(z_w, 1)

            def z_copy(pr):
                act.wait_ge(z_o, 2 * pr + 2)
                a.activation(S["oT"][:, pr, :], bank[6 + pr % 2][:, 0:256], ACT.Copy).then_inc(z_out, 1)
            for h in range(SBH + 3):
                if h < SBH:
                    z_first(h)
                if 0 <= h - 1 < SBH:
                    z_second(h - 1)
                if h >= 3 and h % 2 == 1 and (h - 3) // 2 < 8:
                    z_copy((h - 3) // 2)
            norm(6, H_L1, shift=mcol[:, 72:80])
            silu(1)

        @block.vector
        def _(dve):
            v = nc.vector
            seq = Order(dve, dve_seq)

            def norm(n, gains, dst):
                dve.wait_ge(norm_rs, n + 1)
                for k in range(KT):
                    ins = v.scalar_tensor_tensor(dst[:, k, :], hT[:, k, :], gains[:, k:k + 1], rstd[:, :],
                                                 ALU.mult, ALU.mult)
                    ins.then_inc(norm_out if dst is xn else h_new, 1)

            def read_unit(g, dst):
                dve.wait_ge(unit_done, g + 1)
                v.tensor_copy(dst, bank[g % 2][:, :]).then_inc(unit_out[g % 2], 1)

            v.memset(small[:, 0:4], 0.0).then_inc(rows_used, PRIME)
            dve.wait_ge(x_in, 48)
            v.tensor_tensor(small[:, 4:8], col("lb", 0, 4), col("lb", 4, 4), ALU.subtract).then_inc(lam_a, 1)
            v.tensor_scalar(small[:, 16:20], col("lam", 0, 4), -1.0, None, ALU.mult).then_inc(dve_seq, 1)
            seq.n += 1
            seq.wait()
            v.tensor_tensor(small[:, 20:24], small[:, 16:20], col("lam", 0, 4), ALU.max).then_inc(lam_a, 1)
            norm(0, col("norm1", 0, 8), xn)
            dve.wait_ge(lam_b, 1)
            seq.mark(v.tensor_scalar(small[:, 12:16], small[:, 8:12], -1.0, 1.0, ALU.mult, ALU.add))
            seq.wait()
            wait_unit_out(dve, 2)
            wait_unit_out(dve, 3)
            for h in range(RH):
                v.tensor_scalar(S["fT"][:, h, :], S["fT"][:, h, :], small[:, 12 + h:13 + h], small[:, 8 + h:9 + h],
                                ALU.mult, ALU.add).then_inc(hg_f, 1)
            seq.mark(v.memset(flat(S["D1"]), 1.0))
            seq.wait()
            dve.wait_ge(hg_lf, 1)
            for h in range(RH):
                v.tensor_tensor_scan(S["cum"][:, h, :], S["D1"][:, h, :], S["lf"][:, h, :], 0.0, ALU.mult, ALU.add
                                     ).then_inc(hg_cum, 1)
            dve.wait_ge(hg_cum, 4)
            dve.wait_ge(const_in, 48)

            def level_diff(i):
                b = LEVELS[i]
                cum = flat(S["cum"]).rearrange("p (m two b) -> p m two b", two=2, b=b)
                Dd = flat(S[f"D{i % 2}"]).rearrange("p (m two b) -> p m two b", two=2, b=b)
                ref = cum[:, :, 0, b - 1:b].broadcast_to([P, T * RH // (2 * b), b])
                if i >= 2:
                    dve.wait_ge(hg_kq, 2 * (i - 1))
                v.tensor_tensor(Dd[:, :, 0, :], ref, cum[:, :, 0, :], ALU.subtract).then_inc(hg_d, 1)
                v.tensor_tensor(Dd[:, :, 1, :], cum[:, :, 1, :], ref, ALU.subtract).then_inc(hg_d, 1)

            def level_keep(i):
                dve.wait_ge(hg_ps, i + 1)
                if i == 0:
                    seq.mark(v.tensor_copy(flat(S["ST01"]), bank[2][:, :]))
                    v.memset(S["STd"].rearrange("p a b c -> p (a b c)"), 0.0).then_inc(hg_st, 1)
                    return
                mask = S["masks"][:, i - 1, :].unsqueeze(1).broadcast_to([P, 4, P])
                dve.wait_ge(hg_st, 2 * i - 1)
                for c in range(2):
                    o = S["STd"][:, 2 * c:2 * c + 2, :, :].rearrange("p a b t -> p (a b) t")
                    v.copy_predicated(o, mask, bank[2 + c][:, :].rearrange("p (a t) -> p a t", a=4)
                                      ).then_inc(hg_st, 1)

            def at_logits(i):
                dve.wait_ge(at_s, i + 1)
                if i >= 2:
                    dve.wait_ge(at_p, AT_P[i - 1])
                b = i % 2
                v.tensor_tensor(S[f"L{b}"], bank[4][:, :], S["alibi"][:, i, :], ALU.add).then_inc(at_l, 1)
                dve.wait_ge(at_l, i + 1)
                nh = 2 if i < 4 else 4
                m = S["osm"][:, 8 * b:8 * b + nh]
                if i >= 2:
                    dve.wait_ge(at_pn, AT_P[i - 1])
                seq.mark(v.tensor_reduce(m, S[f"L{b}"].rearrange("p (h k) -> p h k", h=nh), AX.X, ALU.max))
                seq.wait()
                v.tensor_scalar(m, m, -1.0, None, ALU.mult).then_inc(at_mx, 1)

            def at_norm(i):
                nh = 2 if i < 4 else 4
                w = 512 // nh
                b = i % 2
                dve.wait_ge(at_p, AT_P[i + 1])
                s = S["osm"][:, 16 + 8 * b:16 + 8 * b + nh]
                seq.mark(v.reciprocal(s, s))
                seq.wait()
                for h in range(nh):
                    p = S[f"P{b}"][:, h * w:(h + 1) * w]
                    v.tensor_scalar(p, p, s[:, h:h + 1], None, ALU.mult).then_inc(at_pn, 1)

            def at_store(i):
                dve.wait_ge(at_o, i + 1)
                p0 = 64 * (i % 2)
                if i < 4:
                    c = 2 * (i // 2)
                    v.tensor_copy(S["cat"][p0:p0 + 64, c:c + 2, P:T],
                                  bank[6][p0:p0 + 64, 0:T].rearrange("p (a t) -> p a t", a=2)).then_inc(at_cat, 1)
                else:
                    v.tensor_copy(S["cat"][p0:p0 + 64, 0:4, 0:P],
                                  bank[6][p0:p0 + 64, :].rearrange("p (a t) -> p a t", a=4)).then_inc(at_cat, 1)

            AT_P = [0, 2, 4, 6, 8, 12, 16]
            level_diff(0)
            for u in range(4, 14):
                if u in (6, 7):
                    read_unit(u, flat(S["ka"][:, 2 * (u - 6):2 * (u - 6) + 2, :]))
                if u in (8, 9, 10, 11):
                    c = u % 2
                    dst = S["va"] if u < 10 else S["irow"]
                    dve.wait_ge(unit_done, u + 1)
                    v.tensor_copy(dst[:, :, 256 * c:256 * c + 256],
                                  bank[u % 2][:, :].rearrange("p (a n) -> p a n", a=2)).then_inc(unit_out[u % 2], 1)
                i = u - 4
                if i < 7:
                    level_diff(i + 1)
                if i < 8:
                    level_keep(i)
                if i == 8:
                    dve.wait_ge(hg_ps, 9)
                    dve.wait_ge(hg_st, 15)
                    for c in range(2):
                        o = S["STd"][:, 2 * c:2 * c + 2, :, :].rearrange("p a b t -> p (a b) t")
                        m = ident[:, :].bitcast(I32).unsqueeze(1).broadcast_to([P, 4, P])
                        v.copy_predicated(o, m, bank[2 + c][:, :].rearrange("p (a t) -> p a t", a=4)
                                          ).then_inc(hg_st, 1)
                if 0 <= u - 8 < 6:
                    at_logits(u - 8)
                if 0 <= u - 9 < 6:
                    at_norm(u - 9)
                if 0 <= u - 11 < 6:
                    at_store(u - 11)
            at_norm(5)
            for i in (3, 4, 5):
                at_store(i)
            for tt in range(TT):
                dve.wait_ge(rec_ss, tt + 1)
                v.tensor_reduce(S["osm"][:, 32 + 4 * tt:36 + 4 * tt], S["osq"], AX.X, ALU.add).then_inc(rec_var, 1)
            dve.wait_ge(rec_rs, 1)
            wait_unit_out(dve, 12)
            wait_unit_out(dve, 13)
            for tt in range(TT):
                o = S[f"orow{tt}"]
                r = S["osm"][:, 48 + 4 * tt:52 + 4 * tt].unsqueeze(2).broadcast_to([P, RH, P])
                seq.mark(v.tensor_tensor(o, bank[2 + tt][:, :].rearrange("p (h e) -> p h e", h=RH), r, ALU.mult))
                seq.wait()
                v.tensor_tensor(flat(o), flat(o), S["grow"][:, tt, :], ALU.mult).then_inc(rec_row, 1)
            for j in range(4):
                g = UNIT0["outproj"] + j
                dve.wait_ge(unit_done, g + 1)
                h2 = flat(hT[:, 2 * j:2 * j + 2, :])
                v.tensor_tensor(h2, bank[g % 2][:, :], h2, ALU.add).then_inc(h_new, 1)
            norm(1, col("norm2", 0, 8), xn)
            for q in range(4):
                tt, b = q // 2, [2, 3, 6, 7][q]
                dve.wait_ge(hn_t, q + 1)
                v.tensor_copy(S["hnrow"][:, tt, 512 * (q % 2):512 * (q % 2) + 512], bank[b][:, :]
                              ).then_inc(hn_row, 1)

            def top16(vals, work, top, pos, n):
                for i in range(n):
                    last = v.max(top[:, i, 0:8], vals[:, i, :])
                seq.mark(last)
                seq.wait()
                for i in range(n):
                    last = v.match_replace(work[:, i, :], top[:, i, 0:8], vals[:, i, :], -3.0e38)
                    v.max_index(pos[:, i, 0:8], top[:, i, 0:8], vals[:, i, :]) if i < n - 1 else None
                seq.mark(v.max_index(pos[:, n - 1, 0:8], top[:, n - 1, 0:8], vals[:, n - 1, :]))
                seq.wait()
                for i in range(n):
                    last = v.max(top[:, i, 8:16], work[:, i, :])
                seq.mark(last)
                seq.wait()
                for i in range(n):
                    last = v.max_index(pos[:, i, 8:16], top[:, i, 8:16], work[:, i, :])
                return last

            dve.wait_ge(peer_in, 32)
            for tt in range(TT):
                dve.wait_ge(sc_in, 4 * tt + 4)
                v16, i16 = S["v16"], S["i16"]
                top16(S["s"], S["s2"], v16, i16, 16).then_inc(sc_used, 1)
                dve.wait_ge(sc_used, tt + 1)
                seq.mark(v.tensor_copy(flat(S["if16"]), flat(i16)))
                a4 = v16.rearrange("p (h c) i -> p h c i", c=2)
                in0 = a4[:, :, 0, :].unsqueeze(3).broadcast_to([P, PH, 16, 16])
                in1 = a4[:, :, 1, :].unsqueeze(2).broadcast_to([P, PH, 16, 16])
                seq.mark(v.tensor_tensor(S["cand"].rearrange("p h (i j) -> p h i j", i=16), in0, in1, ALU.add))
                seq.wait()
                seq.mark(top16(S["cand"], S["cand2"], S["sc"], S["pos"], PH))
                seq.wait()
                seq.mark(v.tensor_scalar(S["posa"], flat(S["pos"]), 4, None, ALU.logical_shift_right))
                seq.mark(v.tensor_scalar(S["posb"], flat(S["pos"]), 15, None, ALU.bitwise_and))
                seq.wait()
                seq.mark(v.tensor_copy(S["fa"], S["posa"]))
                seq.mark(v.tensor_copy(S["fb"], S["posb"]))
                seq.wait()
                f4 = S["if16"].rearrange("p (h c) i -> p h c i", c=2)
                oh = S["oh"]
                for c, (f, e) in enumerate(((S["fa"], S["e1"]), (S["fb"], S["e2"]))):
                    seq.mark(v.tensor_tensor(oh, f.unsqueeze(2).broadcast_to([P, SLOTS, 16]),
                                             S["iota"].unsqueeze(1).broadcast_to([P, SLOTS, 16]), ALU.is_equal))
                    seq.wait()
                    oh4 = oh.rearrange("p (h k) i -> p h k i", h=PH)
                    seq.mark(v.tensor_tensor(oh4, oh4, f4[:, :, c, :].unsqueeze(2).broadcast_to([P, PH, 16, 16]),
                                             ALU.mult))
                    seq.wait()
                    seq.mark(v.tensor_reduce(e, oh, AX.X, ALU.add))
                    seq.wait()
                seq.mark(v.scalar_tensor_tensor(S["e1"], S["e1"], float(NK), S["e2"], ALU.mult, ALU.add))
                seq.wait()
                v.tensor_copy(S["idx"][:, tt, :], S["e1"]).then_inc(idx_ready, 1)
                g3 = S["gates"][:, tt, :].rearrange("p (h k) -> p h k", h=PH)
                v.tensor_tensor(g3, S["sc"], S["sc"][:, :, 0:1].broadcast_to([P, PH, 16]), ALU.subtract
                                ).then_inc(sc_sub, 1)
                dve.wait_ge(gate_e, tt + 1)
                t8 = S["tiny"][:, 8 * tt:8 * tt + 8]
                seq.mark(v.tensor_reduce(t8, g3, AX.X, ALU.add))
                seq.wait()
                seq.mark(v.reciprocal(t8, t8))
                seq.wait()
                seq.mark(v.tensor_tensor(g3, g3, t8.unsqueeze(2).broadcast_to([P, PH, 16]), ALU.mult))
            for i in range(4):
                seq.mark(v.memset(S["acc"][:, i, :], 0.0))
            seq.wait()
            dve.wait_ge(lam_b, 2)
            seq.mark(v.scalar_tensor_tensor(small[:, 40:44], small[:, 16:20], 0.0, small[:, 28:32], ALU.max, ALU.add))
            seq.wait()
            seq.mark(v.tensor_scalar(small[:, 32:36], small[:, 40:44], 8.0, None, ALU.mult))
            seq.mark(v.tensor_scalar(small[:, 36:40], small[:, 40:44], -8.0, None, ALU.mult))
            seq.mark(v.tensor_scalar(small[:, 44:45], col("qn"), HD ** -0.5, None, ALU.mult))
            for ph in range(4):
                tt, n0 = ph // 2, ph * SLOTS
                if ph % 2 == 0:
                    dve.wait_ge(hn_row, 4)
                    with dve.Fori(0, SLOTS // 16) as it:
                        for j in range(16):
                            n = n0 + j
                            dve.wait_ge(row_in[n % GRING], it * 32 + 16 * (n // GRING + 1))
                            dve.wait_ge(rows_used, it * 16 + (n - 1 + PRIME))
                            v.tensor_tensor_reduce(S["junk"][:, j % 2, :], S["rows"][:, n % GRING, :],
                                                   S["hnrow"][:, tt, :], 1.0, 0.0, ALU.mult, ALU.add,
                                                   S["astage"][:, 0, j:j + 1]).then_inc(rows_used, 1)
                        dve.wait_ge(rows_used, it * 16 + (n0 + 16 + PRIME))
                        v.tensor_copy(S["act"][:, tt, bass.ds(it * 16, 16)], S["astage"][:, 0, :]
                                      ).then_inc(dots_kept, 1)
                        dve.wait_ge(dots_kept, it + (8 * tt + 1))
                    dve.wait_ge(act_gelu, tt + 1)
                    v.tensor_tensor(S["wts"][:, tt, :], S["gel"], S["gates"][:, tt, :], ALU.mult
                                    ).then_inc(wts_ready, 1)
                    dve.wait_ge(wts_ready, tt + 1)
                else:
                    with dve.Fori(0, SLOTS // 16) as it:
                        for j in range(16):
                            n = n0 + j
                            dve.wait_ge(row_in[n % GRING], it * 32 + 16 * (n // GRING + 1))
                            dve.wait_ge(rows_used, it * 16 + (n - 1 + PRIME))
                            acc = S["acc"][:, 2 * tt + j % 2, :]
                            v.scalar_tensor_tensor(acc, S["rows"][:, n % GRING, :],
                                                   S["wts"][:, tt, bass.ds(it * 16 + j, 1)], acc,
                                                   ALU.mult, ALU.add).then_inc(rows_used, 1)
                    dve.wait_ge(rows_used, n0 + SLOTS + PRIME)
                    v.tensor_tensor(S["acc"][:, 2 * tt, :], S["acc"][:, 2 * tt, :], S["acc"][:, 2 * tt + 1, :],
                                    ALU.add).then_inc(acc_ready, 1)
            dve.wait_ge(mcol_ps, 32)
            seq.mark(v.tensor_tensor(mcol[:, :], bank[6][:, 0:96], col("adab", 0, 96), ALU.add))
            seq.wait()
            for i, (n, c) in enumerate((("mix0", 8), ("ffng0", 32), ("mix1", 56), ("ffng1", 80))):
                v.scalar_tensor_tensor(gain[:, i, :], mcol[:, c:c + 8], 1.0, col(n, 0, 8), ALU.add, ALU.mult
                                       ).then_inc(mcol_ready, 1)
            for q in range(4):
                tt, half = q // 2, q % 2
                dve.wait_ge(po_t, q + 1)
                h4 = hT[:, 4 * half:4 * half + 4, tt * P:(tt + 1) * P]
                v.tensor_tensor(h4, bank[2 + q][:, :].rearrange("p (k t) -> p k t", k=4), h4, ALU.add
                                ).then_inc(h_new, 1)
            dve.wait_ge(h_new, H_PEER)
            norm(2, col("normf", 0, 8), hT)
            dve.wait_ge(h_new, H_F)
            dve.wait_ge(mcol_ready, 4)
            norm(3, gain[:, 0, :], xn)
            G0 = UNIT0["l0in"]
            dve.wait_ge(pool_seq, 6)
            wait_unit_out(dve, G0)
            wait_unit_out(dve, G0 + 1)
            for k in range(4):
                for b in range(LH):
                    src = S["rxp"][:, b, k:k + T]
                    w = col("wb", 4 * k + b)
                    if k == 0:
                        ins = v.tensor_scalar(S["xr"][:, b, :], src, w, col("bb", b), ALU.mult, ALU.add)
                    else:
                        ins = v.scalar_tensor_tensor(S["xr"][:, b, :], src, w, S["xr"][:, b, :], ALU.mult, ALU.add)
                    if k == 3:
                        ins.then_inc(xr_ready, 1)
                    else:
                        seq.mark(ins)
                if k < 3:
                    seq.wait()
            for j in (6, 7):
                dve.wait_ge(unit_done, G0 + j + 1)
                wait_unit_out(dve, G0 + j - 2)
                c = 2 * (j - 6)
                v.tensor_tensor(S["prod"][:, c:c + 2, 2:258],
                                bank[(G0 + j) % 2][:, :].rearrange("p (a t) -> p a t", a=2),
                                S["ac"][:, c:c + 2, :], ALU.mult).then_inc(unit_out[(G0 + j) % 2], 1)
            wait_unit_out(dve, G0 + 6)
            wait_unit_out(dve, G0 + 7)
            for k in range(3):
                for b in range(4):
                    src = S["prod"][:, b, k:k + T]
                    w = col("wa", 4 * k + b)
                    if k == 0:
                        ins = v.tensor_scalar(S["cv"][:, b, :], src, w, None, ALU.mult)
                    else:
                        ins = v.scalar_tensor_tensor(S["cv"][:, b, :], src, w, S["cv"][:, b, :], ALU.mult, ALU.add)
                    seq.mark(ins)
                seq.wait()
            for j in (8, 9):
                dve.wait_ge(unit_done, G0 + j + 1)
                c = 2 * (j - 8)
                v.tensor_tensor(flat(S["cat0"][:, c:c + 2, :]), bank[(G0 + j) % 2][:, :],
                                flat(S["cv"][:, c:c + 2, :]), ALU.mult).then_inc(unit_out[(G0 + j) % 2], 1)
            dve.wait_ge(lru_t, 8)
            v.tensor_scalar(flat(S["tT"]), flat(S["tT"]), 1e-18, None, ALU.max).then_inc(lru_c, 1)
            dve.wait_ge(lru_l, 2)
            v.tensor_tensor(flat(S["l1"]), flat(S["l1"]), flat(S["l2"]), ALU.subtract).then_inc(lru_d, 1)
            dve.wait_ge(lru_s, 1)
            dve.wait_ge(lru_ix, 1)
            seq.mark(v.tensor_tensor(flat(S["bT"]), flat(S["l1"]), flat(S["ix"]), ALU.mult))
            seq.wait()
            for b in range(LH):
                seq.mark(v.tensor_tensor_scan(S["hs"][:, b, :], S["aT"][:, b, :], S["bT"][:, b, :], 0.0,
                                              ALU.mult, ALU.add))
            seq.wait()
            v.tensor_tensor(flat(S["cat0"][:, 4:8, :]), flat(S["hs"]), flat(S["gg"]), ALU.mult
                            ).then_inc(cat0_ready, 1)

            def gated_residual(name, m0):
                for j in range(4):
                    g = UNIT0[name] + j
                    dve.wait_ge(unit_done, g + 1)
                    for k in (2 * j, 2 * j + 1):
                        ins = v.scalar_tensor_tensor(hT[:, k, :], bank[g % 2][:, 256 * (k % 2):256 * (k % 2) + 256],
                                                     mcol[:, m0 + k:m0 + k + 1], hT[:, k, :], ALU.mult, ALU.add)
                        ins.then_inc(h_new, 1)

            def swiglu(f, m0):
                G0 = UNIT0[f"ffn{f}"]

                def body(j, u, it):
                    dve.wait_ge(ffn_silu, it * 4 + (FU * f + u + 1))
                    if not isinstance(j, int) or j >= 2:
                        dve.wait_ge(ffn_used, it * 4 + (FU * f + u - 1))
                    v.tensor_tensor(S[f"fa{u % 2}"], S[f"sg{u % 2}"], bank[(G0 + u) % 2][:, 256:512], ALU.mult
                                    ).then_inc(unit_out[(G0 + u) % 2], 1)
                body(0, 0, 0)
                body(1, 1, 0)
                looped(dve, 2, FU, body)
                dve.wait_ge(ffn_used, FU * (f + 1))
                for k in range(KT):
                    v.scalar_tensor_tensor(hT[:, k, :], bank[2 + k // 2][:, 256 * (k % 2):256 * (k % 2) + 256],
                                           mcol[:, m0 + k:m0 + k + 1], hT[:, k, :], ALU.mult, ALU.add
                                           ).then_inc(h_new, 1)
            gated_residual("l0out", 16)
            dve.wait_ge(h_new, H_L0)
            norm(4, gain[:, 1, :], xn)
            swiglu(0, 40)
            dve.wait_ge(h_new, H_FFN0)
            norm(5, gain[:, 2, :], xn)
            for i in range(8):
                dst = flat((S["qT"] if i < 4 else S["kT"])[:, 2 * (i % 4):2 * (i % 4) + 2, :])
                dve.wait_ge(qk_rs, i + 1)
                v.scalar_tensor_tensor(dst, dst, small[:, 44:45] if i < 4 else col("kn"), S["rsh"][:, i % 2, :],
                                       ALU.mult, ALU.mult).then_inc(qk_ready, 1)
            dve.wait_ge(late_in, 64)

            def z_first(h):
                b = h % 2
                z = bank[2 + b][:, 0:384]
                dve.wait_ge(z_ln, h + 1)
                v.scalar_tensor_tensor(S[f"sp{b}"], z, 0.0, S[f"lz{b}"], ALU.max, ALU.add).then_inc(z_sp, 1)
                dve.wait_ge(z_sp, h + 1)
                if h >= 2:
                    dve.wait_ge(z_af, h - 1)
                    dve.wait_ge(z_w, h - 1)
                v.tensor_tensor(S[f"lk{b}"], S[f"sp{b}"], S["sbmask"][:, 0, :], ALU.mult).then_inc(z_lk, 1)
                v.scalar_tensor_tensor(S[f"ls{b}"], z, 1.0, S[f"sp{b}"], ALU.mult, ALU.subtract).then_inc(z_ls, 1)

            def z_second(h):
                b = h % 2
                dve.wait_ge(z_af, h + 1)
                dve.wait_ge(z_ls, h + 1)
                v.tensor_tensor(S[f"ls{b}"], S[f"ls{b}"], bank[4 + b][:, 0:384], ALU.add).then_inc(z_arg, 1)
            for h in range(SBH + 1):
                if h >= 1:
                    z_second(h - 1)
                if h < SBH:
                    z_first(h)
            gated_residual("l1out", 64)
            dve.wait_ge(h_new, H_L1)
            norm(6, gain[:, 3, :], xn)
            swiglu(1, 88)

        @block.tensor
        def _(pe):
            t = nc.tensor

            def norm(n):
                for k in range(KT):
                    pe.wait_ge(norm_sq, 8 * n + k + 1)
                    ins = t.matmul(NORM[:, 0:T], ones[:, :], sq[:, k, :], start=(k == 0), stop=(k == KT - 1))
                ins.then_inc(norm_sum, 1)

            def unit_start(g, it=0, regs=False):
                pe.wait_ge(landed[g % RING], it * 16 + 16 * (g // RING + 1))
                if g >= 2:
                    wait_unit_out(pe, g - 2, it)

            def features(g, src, ready=None):
                w = ring[:, g % RING, 0:2048].rearrange("p (b k c) -> p b k c", b=2, k=KT)
                for b in range(2):
                    for k in range(KT):
                        if ready is not None and b == 0:
                            pe.wait_ge(ready[0], ready[1] + k + 1)
                        ins = t.matmul(bank[g % 2][:, b * T:(b + 1) * T], w[:, b, k, :], src[:, k, :],
                                       start=(k == 0), stop=(k == KT - 1))
                ins.then_inc(unit_done, 1)

            def rows(g, src):
                w = ring[:, g % RING, 0:2048].rearrange("p (b k c) -> p b k c", b=2, k=KT)
                for tt in range(TT):
                    for k in range(KT):
                        ins = t.matmul(bank[g % 2][:, tt * 256:tt * 256 + 256].rearrange("p (b c) -> p b c", b=2),
                                       src[:, k, tt * P:(tt + 1) * P], w[:, :, k, :],
                                       start=(k == 0), stop=(k == KT - 1))
                ins.then_inc(unit_done, 1)

            pe.wait_ge(x_in, 48)
            norm(0)

            def level(i):
                if i < 8:
                    pe.wait_ge(hg_kq, 2 * i + 2)
                if i > 0:
                    pe.wait_ge(hg_st, 2 * i - 1)
                if i < 8:
                    kd, qd = S[f"K{i % 2}"], S[f"Q{i % 2}"]
                else:
                    kd, qd = S["kk"], S["qf"]
                for h in range(RH):
                    if i == 0:
                        ins = t.matmul(bank[2][:, h * P:(h + 1) * P], kd[:, h, 0:P], qd[:, h, P:T],
                                       start=True, stop=True)
                        continue
                    for tt in range(TT):
                        at = (2 * (h % 2) + tt) * P
                        ins = t.matmul(bank[2 + h // 2][:, at:at + P], kd[:, h, tt * P:(tt + 1) * P],
                                       qd[:, h, tt * P:(tt + 1) * P], start=True, stop=True)
                ins.then_inc(hg_ps, 1)

            def at_scores(i):
                if i == 0:
                    for g in (4, 5, 6, 7):
                        wait_unit_out(pe, g)
                else:
                    pe.wait_ge(at_l, i)
                for c in range(2 if i < 4 else 4):
                    h = at_head(i, c)
                    p0 = 64 * (h % 2)
                    n = T if i < 4 else P
                    q0 = P if i < 4 else 0
                    ins = t.matmul(bank[4][:, c * n:(c + 1) * n], S["qa"][p0:p0 + 64, h // 2, q0:q0 + P],
                                   S["ka"][p0:p0 + 64, h // 2, 0:n], start=True, stop=True)
                ins.then_inc(at_s, 1)

            AT_P = [0, 2, 4, 6, 8, 12, 16]

            def at_transpose(i):
                pe.wait_ge(at_pn, AT_P[i + 1])
                if i:
                    pe.wait_ge(at_pt, i)
                for c in range(4):
                    ins = t.transpose(bank[5][:, c * P:(c + 1) * P], S[f"P{i % 2}"][:, c * P:(c + 1) * P],
                                      ident[:, :])
                ins.then_inc(at_t, 1)

            def at_out(i):
                pe.wait_ge(at_pt, i + 1)
                if i == 0:
                    wait_unit_out(pe, 8)
                    wait_unit_out(pe, 9)
                else:
                    pe.wait_ge(at_cat, i)
                pt = S[f"PT{i % 2}"]
                p0 = 64 * (i % 2)
                for c in range(2 if i < 4 else 4):
                    h = at_head(i, c)
                    for kt in range(2 if i < 4 else 1):
                        ins = t.matmul(bank[6][p0:p0 + 64, c * P:(c + 1) * P], S["va"][:, kt, h * HD:(h + 1) * HD],
                                       pt[:, 2 * c + kt if i < 4 else c, :], start=(kt == 0), stop=(i >= 4 or kt == 1))
                ins.then_inc(at_o, 1)

            pe.wait_ge(const_in, 48)
            for u in range(14):
                unit_start(u)
                if u < 8:
                    features(u, xn, (norm_out, 0) if u == 0 else None)
                else:
                    rows(u, xn)
                if u >= 4 and u - 4 < 9:
                    level(u - 4)
                if 0 <= u - 8 < 6:
                    at_scores(u - 8)
                if 0 <= u - 9 < 6:
                    at_transpose(u - 9)
                if 0 <= u - 10 < 6:
                    at_out(u - 10)
            at_transpose(5)
            at_out(4)
            pe.wait_ge(hg_st, 17)
            wait_unit_out(pe, 10)
            wait_unit_out(pe, 11)
            for tt in range(TT):
                for h in range(RH):
                    o = bank[2 + tt][:, h * P:(h + 1) * P]
                    if tt:
                        t.matmul(o, S["ST01"][:, h, :], S["irow"][:, 0, h * P:(h + 1) * P], start=True, stop=False)
                    ins = t.matmul(o, S["STd"][:, h, tt, :], S["irow"][:, tt, h * P:(h + 1) * P],
                                   start=(tt == 0), stop=True)
                ins.then_inc(rec_o, 1)
            at_out(5)
            for tt in range(TT):
                pe.wait_ge(rec_row, tt + 1)
                if tt == 0:
                    pe.wait_ge(at_l, 6)
                else:
                    pe.wait_ge(at_pt, 6)
                for h in range(RH):
                    ins = t.transpose(bank[4 + tt][:, h * P:(h + 1) * P], S[f"orow{tt}"][:, h, :], ident[:, :])
                ins.then_inc(rec_t, 1)
            pe.wait_ge(at_cat, 6)
            pe.wait_ge(rec_cat, 8)
            for j in range(4):
                g = UNIT0["outproj"] + j
                unit_start(g)
                features(g, S["cat"])
            norm(1)
            for j in range(8):
                g = UNIT0["peerq"] + j
                unit_start(g)
                features(g, xn, (norm_out, 8) if j == 0 else None)
            for q in range(4):
                tt, b = q // 2, [2, 3, 6, 7][q]
                for k in range(4):
                    ins = t.transpose(bank[b][:, k * P:(k + 1) * P],
                                      xn[:, 4 * (q % 2) + k, tt * P:(tt + 1) * P], ident[:, :])
                ins.then_inc(hn_t, 1)
            wait_unit_out(pe, UNIT0["peerq"] + 6)
            wait_unit_out(pe, UNIT0["peerq"] + 7)
            pe.wait_ge(peer_in, 32)
            pe.wait_ge(hn_row, 2)
            for q in range(8):
                tt = q // 4
                if q >= 4:
                    pe.wait_ge(sc_in, q - 3)
                for c in range(4):
                    hc = 4 * (q % 4) + c
                    ins = t.matmul(bank[[4, 5, 2, 3][q % 4]][:, c * P:(c + 1) * P],
                                   S["qpT"][:, hc, tt * P:(tt + 1) * P], S["subk"][:, hc, :], start=True, stop=True)
                ins.then_inc(sc_ps, 1)
            pe.wait_ge(silc_ready, 1)
            pe.wait_ge(hn_row, 4)
            G0 = UNIT0["ada"]

            def ada_unit(j, u, it):
                g = G0 + u
                pe.wait_ge(landed[g % RING], it * 16 + 16 * (g // RING + 1))
                wait_unit_out(pe, g - 2, it)
                w = ring[:, g % RING, :].rearrange("p (k c) -> p k c", k=KT)
                for k in range(KT):
                    ins = t.matmul(bank[g % 2][0:1, 0:ADA_COLS], silc[:, k:k + 1], w[:, k, :],
                                   start=(k == 0), stop=(k == KT - 1))
                ins.then_inc(unit_done, 1)

            def ada_column(j, u, it):
                wait_unit_out(pe, G0 + u, it)
                for c in range(3):
                    at = j * 3 + c
                    o = bank[6][:, at:at + 1] if isinstance(at, int) else bank[6][:, bass.ds(at, 1)]
                    ins = t.matmul(o, S["mrow"][0:1, u % 2, c * P:(c + 1) * P], ones[0:1, 0:1], start=True, stop=True)
                ins.then_inc(mcol_ps, 1)
            ada_unit(0, 0, 0)

            def both(j, u, it):
                ada_unit(j, u, it)
                ada_column(j - 1, u - 1, it)
            looped(pe, 1, 32, both)
            ada_column(31, 31, 0)
            for q in range(4):
                tt, half = q // 2, q % 2
                pe.wait_ge(acc_ready, tt + 1)
                for k in range(4):
                    at = (4 * half + k) * P
                    ins = t.transpose(bank[2 + q][:, k * P:(k + 1) * P], S["acc"][:, 2 * tt, at:at + P], ident[:, :])
                ins.then_inc(po_t, 1)
            norm(2)
            norm(3)
            G0 = UNIT0["l0in"]
            for j in range(10):
                unit_start(G0 + j)
                features(G0 + j, xn, (norm_mod, 0) if j == 0 else None)
                if j == 4:
                    pe.wait_ge(late_in, 16)
                    pe.wait_ge(xr_ready, 4)
                    for b in range(8):
                        ins = t.matmul(bank[2 + b // 2][:, 256 * (b % 2):256 * (b % 2) + 256], S["rgw"][:, b, :],
                                       S["xr"][:, b % 4, :], start=True, stop=True)
                        if b % 2:
                            ins.then_inc(rg_ps, 1)
            wait_unit_out(pe, G0 + 8)
            wait_unit_out(pe, G0 + 9)
            pe.wait_ge(cat0_ready, 1)
            for j in range(4):
                unit_start(UNIT0["l0out"] + j)
                features(UNIT0["l0out"] + j, S["cat0"])
            norm(4)

            def swiglu(f):
                G0 = UNIT0[f"ffn{f}"]

                def gate_up(j, u, it):
                    g = G0 + u
                    pe.wait_ge(landed[g % RING], it * 16 + 16 * (g // RING + 1))
                    wait_unit_out(pe, g - 2, it)
                    w = ring[:, g % RING, 0:2048].rearrange("p (b k c) -> p b k c", b=2, k=KT)
                    for b in range(2):
                        for k in range(KT):
                            if isinstance(j, int) and j == 0 and b == 0:
                                pe.wait_ge(norm_mod, 8 * (1 + 2 * f) + k + 1)
                            ins = t.matmul(bank[g % 2][:, b * T:(b + 1) * T], w[:, b, k, :], xn[:, k, :],
                                           start=(k == 0), stop=(k == KT - 1))
                    ins.then_inc(unit_done, 1)

                def down(j, u, it):
                    g = G0 + u
                    wait_unit_out(pe, g, it)
                    w = ring[:, g % RING, 2048:3072].rearrange("p (n c) -> p n c", n=KT)
                    first = isinstance(j, int) and j == 0
                    last = isinstance(j, int) and j == FU - 1
                    for n in range(KT):
                        ins = t.matmul(bank[2 + n // 2][:, 256 * (n % 2):256 * (n % 2) + 256], w[:, n, :],
                                       S[f"fa{u % 2}"], start=(first and n % 2 == 0), stop=last,
                                       skip_group_check=True)
                    ins.then_inc(ffn_used, 1)

                def both(j, u, it):
                    gate_up(j, u, it)
                    down(j - 1, u - 1, it)
                gate_up(0, 0, 0)
                both(1, 1, 0)
                looped(pe, 2, FU, both)
                down(FU - 1, FU - 1, 0)
            swiglu(0)
            norm(5)
            G0 = UNIT0["qkv"]

            def qk_sums(i):
                pe.wait_ge(qk_sq, i + 1)
                if i >= 2:
                    pe.wait_ge(qk_rs, i - 1)
                t.matmul(bank[2 + i % 2][:, :], S["blk"], S["sqh"][:, i % 2, :], start=True, stop=True
                         ).then_inc(qk_sum, 1)
            for j in range(12):
                unit_start(G0 + j)
                if j < 8:
                    features(G0 + j, xn, (norm_mod, 16) if j == 0 else None)
                else:
                    rows(G0 + j, xn)
                if j == 0:
                    pe.wait_ge(late_in, 64)
                if 1 <= j <= 8:
                    qk_sums(j - 1)
            pe.wait_ge(qk_rs, 8)
            wait_unit_out(pe, G0 + 10)
            wait_unit_out(pe, G0 + 11)

            def z_scores(h):
                if h == 0:
                    pe.wait_ge(qk_ready, 8)
                if h >= 2:
                    pe.wait_ge(z_ls, h - 1)
                p0, pr = 64 * (h % 2), h // 2
                q, k = S["qT"][p0:p0 + 64, pr, :], S["kT"][p0:p0 + 64, pr, :]
                o = bank[2 + h % 2]
                t.matmul(o[:, 0:T], k[:, 0:P], q, start=True, stop=True)
                t.matmul(o[:, T:T + P], k[:, P:T], q[:, P:T], start=True, stop=True).then_inc(z_ps, 1)

            def z_after(h):
                pe.wait_ge(z_lk, h + 1)
                if h >= 2:
                    pe.wait_ge(z_arg, h - 1)
                o, lk = bank[4 + h % 2], S[f"lk{h % 2}"]
                t.matmul(o[:, 0:T], S["tri"], lk[:, 0:T], start=True, stop=False, skip_group_check=True)
                t.matmul(o[:, P:T], ones[:, :], lk[:, T:T + P], start=False, stop=True, skip_group_check=True)
                t.matmul(o[:, T:T + P], S["tri"], lk[:, T:T + P], start=True, stop=True, skip_group_check=True
                         ).then_inc(z_af, 1)

            def z_value(h):
                pe.wait_ge(z_wm, h + 1)
                pr = h // 2
                if h % 2 == 0 and pr >= 2:
                    pe.wait_ge(z_out, pr - 1)
                o = bank[6 + pr % 2][64 * (h % 2):64 * (h % 2) + 64, :]
                w = S[f"wz{h % 2}"]
                t.matmul(o[:, 0:T], S["vrow"][:, 0, h * HD:(h + 1) * HD], w[:, 0:T], start=True, stop=False,
                         skip_group_check=True)
                t.matmul(o[:, P:T], S["vrow"][:, 1, h * HD:(h + 1) * HD], w[:, T:T + P], start=False, stop=True,
                         skip_group_check=True).then_inc(z_o, 1)
            for h in range(SBH + 2):
                if h < SBH:
                    z_scores(h)
                if 0 <= h - 1 < SBH:
                    z_after(h - 1)
                if 0 <= h - 2 < SBH:
                    z_value(h - 2)
            pe.wait_ge(z_out, 8)
            for j in range(4):
                unit_start(UNIT0["l1out"] + j)
                features(UNIT0["l1out"] + j, S["oT"])
            norm(6)
            swiglu(1)


def tiles(w):
    n = w.shape[1] // 256
    return w.reshape(8, 128, n, 2, 128).transpose(2, 1, 3, 0, 4).reshape(n, 128, 2048)


def ffn_tiles(gate, up, down):
    n = gate.shape[1] // 128
    g, u = (w.reshape(8, 128, n, 128).transpose(2, 1, 0, 3).reshape(n, 128, 1024) for w in (gate, up))
    return np.concatenate([g, u, down.reshape(n, 128, 1024)], axis=2)


def layout(I):
    w = {}
    inp = tiles(I["w_in"][0])
    w["inproj"] = inp[[6, 7, 8, 9, 0, 1, 2, 3, 4, 5, 10, 11, 12, 13]]
    w["outproj"] = tiles(I["w_out"][0])
    w["peerq"] = tiles(I["peer_wq"][0])
    ada = [I[f"l{i}_ada_w_2"].reshape(8, 128, 16, 384).transpose(2, 1, 0, 3).reshape(16, 128, 3072) for i in (0, 1)]
    w["ada"] = np.concatenate(ada, axis=0)
    w["l0in"] = tiles(I["l0_w_in_2"])[[8, 9, 6, 7, 2, 3, 4, 5, 0, 1]]
    w["l0out"] = tiles(I["l0_w_out_2"])
    w["ffn0"] = ffn_tiles(*(I[f"l0_ffn_w_{n}_2"] for n in ("gate", "up", "down")))
    w["qkv"] = tiles(I["l1_w_qkv_2"])
    w["l1out"] = tiles(I["l1_w_out_2"])
    w["ffn1"] = ffn_tiles(*(I[f"l1_ffn_w_{n}_2"] for n in ("gate", "up", "down")))

    def fm(v):
        return v.reshape(-1, 128).T
    c = {"norm1": fm(I["norm1_g"]), "norm2": fm(I["norm2_g"]), "normf": fm(I["normf_g"]),
         "lb": fm(I["rec_lb_logits"]), "recg": fm(I["rec_norm_g"]), "c": fm(I["c_2"]),
         "adab": np.concatenate([fm(I["l0_ada_b_2"]), fm(I["l1_ada_b_2"])], axis=1),
         "mix0": fm(I["l0_mix_norm_2"]), "ffng0": fm(I["l0_ffn_norm_2"]), "mix1": fm(I["l1_mix_norm_2"]),
         "ffng1": fm(I["l1_ffn_norm_2"]), "wa": fm(I["l0_conv_a_w_2"]), "wb": fm(I["l0_conv_b_w_2"]),
         "bb": fm(I["l0_conv_b_b_2"]), "ba": fm(I["l0_rg_a_b_2"]), "bx": fm(I["l0_rg_x_b_2"]),
         "lam": fm(I["l0_rg_lambda_2"]), "qn": np.tile(I["l1_q_norm_2"], 2).reshape(128, 1),
         "kn": np.tile(I["l1_k_norm_2"], 2).reshape(128, 1), "one": np.full((128, 1), 1.0, np.float32),
         "eps": np.full((128, 1), EPS, np.float32)}
    a = {f"w_{k}": v for k, v in w.items()}
    a["xT"] = I["x"][0].T.reshape(8, 128, 256).transpose(1, 0, 2)
    a["cols_d"] = np.concatenate([c[n] for n, _ in COLS], axis=1)
    a["subk_d"] = I["peer_subkeys"][0].reshape(16, 128, 128).transpose(2, 0, 1)
    rg = np.zeros((128, 8, 128), np.float32)
    for i, n in enumerate(("l0_rg_a_w_2", "l0_rg_x_w_2")):
        for h in range(8):
            s = 64 * (h % 2)
            rg[s:s + 64, 4 * i + h // 2, s:s + 64] = I[n][h]
    a["rg_d"] = rg
    a["u_d"], a["v_d"] = I["peer_u"][0], I["peer_v"][0]
    return {k: np.ascontiguousarray(v) for k, v in a.items()}


def constants():
    q, k = np.arange(256)[:, None], np.arange(256)[None, :]
    alibi = np.zeros((128, 6, 512), np.float32)
    for i in range(6):
        for c in range(2 if i < 4 else 4):
            slope = np.float32(2.0 ** (-8.0 * (at_head(i, c) + 1) / HEADS))
            bias = np.where(k <= q, -slope * (q - k).astype(np.float32), np.float32(NEG)).astype(np.float32)
            if i < 4:
                alibi[:, i, 256 * c:256 * c + 256] = bias[128:]
            else:
                alibi[:, i, 128 * c:128 * c + 128] = bias[:128, :128]
    s, t = np.arange(128)[:, None], np.arange(128)[None, :]
    masks = np.stack([((s // b) % 2 == 0) & (t // b == s // b + 1) for b in LEVELS[1:]], axis=1).astype(np.int32)
    before = (s < t).astype(np.float32)
    full = np.ones((128, 128), np.float32)
    sbm = np.stack([np.concatenate([-before, -full, -before], axis=1),
                    np.concatenate([before, full, before], axis=1)], axis=1)
    half = (s // 64 == t // 64).astype(np.float32)
    return {"alibi_d": alibi, "masks_d": masks, "ident_d": np.eye(128, dtype=np.float32),
            "tri_d": (s > t).astype(np.float32), "blk_d": half, "sbmask_d": sbm,
            "iota_d": np.tile(np.arange(16, dtype=np.float32), (128, 1))}


def kernel(**inputs):
    import concourse.bacc as _bacc
    from concourse.bass_utils import run_bass_kernel_spmd as _run

    nc = _bacc.Bacc("TRN2", target_bir_lowering=False, num_devices=1)
    arrays = layout({k: np.asarray(v) for k, v in inputs.items()})
    arrays.update(constants())
    aps = {n: nc.dram_tensor(n, a.shape, mybir.dt.from_np(a.dtype), kind="ExternalInput").ap()
           for n, a in arrays.items()}
    weights = {n[2:]: aps.pop(n) for n in list(aps) if n.startswith("w_")}
    out = nc.dram_tensor("out", (128, 8, 256), F32, kind="ExternalOutput").ap()
    build(nc, w_d=weights, out=out, **aps)
    r = _run(nc, [arrays], core_ids=[0])
    return np.ascontiguousarray(r.results[0]["out"].transpose(1, 0, 2).reshape(1024, 256).T[None])
```

```python
from contextlib import ExitStack

import numpy as np

import concourse.bass as bass
from concourse import mybir

F32 = mybir.dt.float32
F32R = mybir.dt.float32r
I32 = mybir.dt.int32
U32 = mybir.dt.uint32
ALU = mybir.AluOpType
ACT = mybir.ActivationFunctionType
AX = mybir.AxisListType

P = 128
D = 1024
T = 256
KT = D // P
TT = T // P
HEADS, HD = 8, 64
RH = 4
PH, NK, TOPK = 8, 128, 16
SLOTS = PH * TOPK
FF = 2816
FU = FF // P
LH, LW = 4, 512
SBH = 16
EPS = 1e-6
NEG = -1e30

LAYERS = [("inproj", 14), ("outproj", 4), ("peerq", 8), ("ada", 32), ("l0in", 10), ("l0out", 4),
          ("ffn0", FU), ("qkv", 12), ("l1out", 4), ("ffn1", FU)]
UNIT0, UNITS = {}, {}
_at = 0
for _name, _n in LAYERS:
    UNIT0[_name], UNITS[_name] = _at, _n
    _at += _n
UNIT_COLS = {"ada": 3072, "ffn0": 3072, "ffn1": 3072}
RING = 4
RING_COLS = 3072
ADA_COLS = 384
GRING = 8
SPLIT0 = UNIT0["l0in"]
PRIME = 32

COLS = [("norm1", 8), ("norm2", 8), ("normf", 8), ("lb", 8), ("recg", 4), ("c", 8), ("adab", 96),
        ("mix0", 8), ("ffng0", 8), ("mix1", 8), ("ffng1", 8), ("wa", 12), ("wb", 16), ("bb", 4),
        ("ba", 4), ("bx", 4), ("lam", 4), ("qn", 1), ("kn", 1), ("one", 1), ("eps", 1)]
COL = {}
_at = 0
for _name, _n in COLS:
    COL[_name] = (_at, _n)
    _at += _n
NCOLS = _at
LEVELS = [128, 64, 32, 16, 8, 4, 2, 1]


def at_head(i, c):
    return 4 * (i // 2) + i % 2 + 2 * c if i < 4 else (i - 4) + 2 * c


def build(nc, xT, cols_d, w_d, alibi_d, masks_d, ident_d, tri_d, blk_d, sbmask_d, iota_d, subk_d, rg_d,
          u_d, v_d, out):
    with ExitStack() as ctx:
        def sb(name, shape, dt=F32):
            return ctx.enter_context(nc.sbuf_tensor(name, shape, dt))

        def sem(name):
            return ctx.enter_context(nc.semaphore(name))

        bank = [ctx.enter_context(nc.psum_tensor(f"bank{i}", [P, 512], F32)) for i in range(8)]
        NORM = bank[7]

        ring = sb("ring", [P, RING, RING_COLS])
        hT = sb("hT", [P, KT, T])
        sq = sb("sq", [P, KT, T])
        rstd = sb("rstd", [P, T])
        lnv = sb("lnv", [P, T])
        cols = sb("cols", [P, NCOLS])
        ones = sb("ones", [P, P])
        ident = sb("ident", [P, P])
        mcol = sb("mcol", [P, 96])
        gain = sb("gain", [P, 4, 8])
        silc = sb("silc", [P, 8])
        small = sb("small", [P, 64])
        S = {}
        ARENA = 32000
        first = ExitStack()
        xn = first.enter_context(nc.sbuf_tensor("xn", [P, KT, T], F32))
        arena = first.enter_context(nc.sbuf_tensor("arena", [P, ARENA], F32))

        def place(base, items, on=arena):
            at, arena = base, on
            for name, shape, *dt in items:
                n = int(np.prod(shape))
                v = arena[:, at:at + n]
                if dt:
                    v = v.bitcast(dt[0])
                if len(shape) == 2:
                    v = v.rearrange("p (a b) -> p a b", b=shape[1])
                elif len(shape) == 3:
                    v = v.rearrange("p (a b c) -> p a b c", b=shape[1], c=shape[2])
                S[name] = v
                at += n
            assert at <= on.shape[1], (at, items[0][0])
            return at

        place(0, [("qf", (4, 256)), ("fT", (4, 256)), ("lf", (4, 256)), ("kk", (4, 256)), ("cum", (4, 256)),
                  ("D0", (4, 256)), ("D1", (4, 256)), ("K0", (4, 256)), ("K1", (4, 256)),
                  ("Q0", (4, 256)), ("Q1", (4, 256)), ("irow", (2, 512)), ("grow", (2, 512)),
                  ("qa", (4, 256)), ("ka", (4, 256)), ("va", (2, 512)), ("STd", (4, 2, 128)), ("ST01", (4, 128)),
                  ("L0", (512,)), ("L1", (512,)), ("P0", (512,)), ("P1", (512,)), ("PT0", (4, 128)), ("PT1", (4, 128)),
                  ("alibi", (6, 512)), ("masks", (7, 128), I32), ("osq", (4, 128)), ("orow0", (4, 128)),
                  ("orow1", (4, 128)), ("osm", (64,)), ("cat", (8, 256))])
        place(0, [("qpT", (16, 256)), ("hnrow", (2, 1024)), ("rows", (GRING, 1024)), ("junk", (2, 1024)),
                  ("idx", (2, 128), I32), ("gates", (2, 128)), ("act", (2, 128)), ("gel", (128,)),
                  ("wts", (2, 128)), ("istage", (2, 16), I32), ("astage", (2, 16)), ("tiny", (64,)),
                  ("mrow", (2, 384)), ("s", (16, 128)), ("s2", (16, 128)),
                  ("v16", (16, 16)), ("i16", (16, 16), U32), ("if16", (16, 16)), ("cand", (8, 256)),
                  ("cand2", (8, 256)), ("sc", (8, 16)), ("pos", (8, 16), U32), ("posa", (128,), U32),
                  ("posb", (128,), U32), ("fa", (128,)), ("fb", (128,)), ("e1", (128,)),
                  ("e2", (128,)), ("subk", (16, 128)), ("iota", (16,))])
        S["acc"] = arena[:, 0:4096].rearrange("p (a b) -> p a b", b=1024)
        S["oh"] = S["s2"].rearrange("p a b -> p (a b)").rearrange("p (a b) -> p a b", b=16)
        first.close()
        xh = sb("xh", [P, KT, T])
        second = sb("second", [P, 12544])
        for n, shape in [(f"{n}{i}", [P, 256]) for i in (0, 1) for n in ("fh", "fl")] + \
                        [("yh", [P, KT, T]), ("yl", [P, KT, T]), ("xl", [P, KT, T])] + \
                        [(f"{n}{i}", [P, 2048]) for i in (0, 1) for n in ("whi", "wlo")] + \
                        [(f"{n}{i}", [P, 1024]) for i in (0, 1) for n in ("dhi", "dlo")]:
            tensor = sb(n, shape)
            S[n] = tensor[:, :, :] if len(shape) == 3 else tensor[:, :]
        xl = S["xl"]
        place(0, [("rxp", (4, 259)), ("gg", (4, 256)), ("ac", (4, 256)), ("prod", (4, 258)), ("xr", (4, 256)),
                  ("cv", (4, 256)), ("rT", (4, 256)), ("iT", (4, 256)), ("aT", (4, 256)), ("tT", (4, 256)),
                  ("l1", (4, 256)), ("rgw", (8, 128))], second)
        S["ix"], S["l2"], S["bT"], S["hs"] = S["iT"], S["rT"], S["l1"], S["tT"]
        place(0, [(f"{n}{i}", (256,)) for i in (0, 1) for n in ("sg", "fa")], second)
        place(0, [("qT", (8, 256)), ("kT", (8, 256)), ("vrow", (2, 1024))] +
                 [(f"{n}{i}", (384,)) for n in ("az", "ez", "lz", "sp", "lk", "ls", "wz") for i in (0, 1)] +
                 [("tri", (128,)), ("blk", (128,)), ("sbmask", (2, 384))], second)
        place(6144, [("rsh", (8, 512)), ("sqh", (2, 512))], second)
        S["cat0h"] = S["oTh"] = S["yh"]
        S["cat0l"] = S["oTl"] = S["yl"]

        def r32(ap):
            return ap.bitcast(F32R)

        def col(name, i=0, n=1):
            return cols[:, COL[name][0] + i:COL[name][0] + i + n]

        x_in = sem("x_in")
        const_in = sem("const_in")
        peer_in = sem("peer_in")
        late_in = sem("late_in")
        landed = [sem(f"landed{i}") for i in range(RING)]
        unit_done = sem("unit_done")
        unit_out = [sem(f"unit_out{i}") for i in range(2)]
        ffn_used = sem("ffn_used")
        ffn_silu = sem("ffn_silu")
        bank_full = sem("bank_full")
        norm_sq, norm_sum, norm_rs, norm_out = (sem(n) for n in (
            "norm_sq", "norm_sum", "norm_rs", "norm_out"))
        h_new = sem("h_new")
        dve_seq, act_seq, pool_seq = sem("dve_seq"), sem("act_seq"), sem("pool_seq")
        hg_f, hg_lf, hg_kk, hg_cum, hg_d, hg_e, hg_kq, hg_ps, hg_st = (sem(n) for n in (
            "hg_f", "hg_lf", "hg_kk", "hg_cum", "hg_d", "hg_e", "hg_kq", "hg_ps", "hg_st"))
        rec_o, rec_ss, rec_var, rec_rs, rec_row, rec_t, rec_cat = (sem(n) for n in (
            "rec_o", "rec_ss", "rec_var", "rec_rs", "rec_row", "rec_t", "rec_cat"))
        at_s, at_l, at_mx, at_p, at_pn, at_t, at_pt, at_o, at_cat = (sem(n) for n in (
            "at_s", "at_l", "at_mx", "at_p", "at_pn", "at_t", "at_pt", "at_o", "at_cat"))
        hn_t, hn_row, sc_ps, sc_in, sc_used, idx_ready, sc_sub, gate_e, dots_kept, act_gelu, wts_ready, acc_ready, po_t = (
            sem(n) for n in ("hn_t", "hn_row", "sc_ps", "sc_in", "sc_used", "idx_ready", "sc_sub", "gate_e",
                             "dots_kept", "act_gelu", "wts_ready", "acc_ready", "po_t"))
        row_in = [sem(f"row_in{i}") for i in range(GRING)]
        rows_used = sem("rows_used")
        staged = sem("staged")
        waited = sem("waited")
        silc_ready, mcol_ps, mcol_ready, lam_a, lam_b = (sem(n) for n in (
            "silc_ready", "mcol_ps", "mcol_ready", "lam_a", "lam_b"))
        xr_ready, rg_ps, rg_sig, lru_t, lru_c, lru_l, lru_d, lru_s, lru_ix, cat0_ready = (sem(n) for n in (
            "xr_ready", "rg_ps", "rg_sig", "lru_t", "lru_c", "lru_l", "lru_d", "lru_s", "lru_ix", "cat0_ready"))
        cat0_full, cat0_hi, z_lo = sem("cat0_full"), sem("cat0_hi"), sem("z_lo")
        w_hi, w_lo, d_hi, d_lo, x_hi, x_lo, f_full, f_hi, f_lo = (sem(n) for n in (
            "w_hi", "w_lo", "d_hi", "d_lo", "x_hi", "x_lo", "f_full", "f_hi", "f_lo"))
        qk_sq, qk_sum, qk_ln, qk_rs, qk_ready, z_ps, z_ln, z_sp, z_ls, z_lk, z_af, z_arg, z_w, z_wm, z_o, z_out = (sem(n) for n in (
            "qk_sq", "qk_sum", "qk_ln", "qk_rs", "qk_ready", "z_ps", "z_ln", "z_sp", "z_ls", "z_lk", "z_af", "z_arg", "z_w", "z_wm",
            "z_o", "z_out"))
        stored = sem("stored")

        class Order:

            def __init__(self, eng, s):
                self.eng, self.s, self.n = eng, s, 0

            def mark(self, ins):
                ins.then_inc(self.s, 1)
                self.n += 1
                return self.n

            def wait(self, n=None):
                self.eng.wait_ge(self.s, self.n if n is None else n)

        H_MIX, H_PEER, H_F, H_L0, H_FFN0, H_L1, H_FINAL = 4, 8, 16, 24, 32, 40, 48

        def wait_unit_out(eng, g, it=0):
            for name, base, per in (("outproj", 0, 1), ("l0out", H_F, 2), ("l1out", H_FFN0, 2)):
                if UNIT0[name] <= g < UNIT0[name] + UNITS[name]:
                    eng.wait_ge(h_new, base + per * (g - UNIT0[name] + 1))
                    return
            for f in (0, 1):
                j = g - UNIT0[f"ffn{f}"]
                if 0 <= j < FU:
                    eng.wait_ge(f_full, it * 4 + (FU * f + j + 1))
                    return
            joined = sum(1 for n in ("outproj", "l0out", "ffn0", "l1out") for j in range(UNITS[n])
                         if UNIT0[n] + j <= g and (UNIT0[n] + j) % 2 == g % 2)
            eng.wait_ge(unit_out[g % 2], it * 2 + (g // 2 + 1 - joined))

        def down_done(f, j):
            return (FU - 1) * f + j + 1

        def looped(eng, lo, hi, body):
            n = (hi - lo) // 4
            with eng.Fori(0, n) as it:
                for u in range(4):
                    body(it * 4 + (lo + u), lo + u, it)
            for j in range(lo + 4 * n, hi):
                body(j, j, 0)

        def flat(ap):
            return ap.rearrange("p a b -> p (a b)")


        block = ctx.enter_context(nc.Block())

        @block.sync
        def _(sp):
            def load(u, g, src, it=0):
                sp.dma_start(ring[:, g % RING, 0:src.shape[-1]], src).then_inc(landed[g % RING], 16)

            def wait_slot(g, it=0):
                b = g - RING
                if b < 0:
                    return
                if b >= SPLIT0:
                    for f, k in (("ffn0", 0), ("ffn1", 1)):
                        if UNIT0[f] <= b < UNIT0[f] + FU:
                            sp.wait_ge(d_lo, it * 4 + (b - UNIT0[f] + 1 + FU * k))
                            return
                    sp.wait_ge(w_lo, it * 4 + (b - SPLIT0 + 1))
                    return
                sp.wait_ge(unit_done, it * 4 + (b + 1))

            sp.dma_start(cols[:, :], cols_d).then_inc(x_in, 16)
            sp.dma_start(hT[:, :, :], xT).then_inc(x_in, 16)
            for j in range(UNITS["inproj"]):
                wait_slot(j)
                load(0, j, w_d["inproj"][j])
            for name in ("outproj", "peerq"):
                g0 = UNIT0[name]
                for j in range(UNITS[name]):
                    wait_slot(g0 + j)
                    load(0, g0 + j, w_d[name][j])
            for name in ("ada", "l0in", "l0out", "ffn0", "qkv", "l1out", "ffn1"):
                g0, n = UNIT0[name], UNITS[name]
                for j in range(4):
                    wait_slot(g0 + j)
                    load(0, g0 + j, w_d[name][j])

                def body(j, u, it):
                    wait_slot(g0 + u, it)
                    load(0, g0 + u, w_d[name][j])
                if n > 4:
                    looped(sp, 4, n, body)
            sp.wait_ge(h_new, H_FINAL)
            sp.dma_start(out, hT[:, :, :]).then_inc(stored, 16)
            sp.wait_ge(stored, 16)


        @block.gpsimd
        def _(pool):
            seq = Order(pool, pool_seq)
            g = nc.gpsimd
            g.memset(ones[:, :], 1.0).then_inc(x_in, 16)
            g.dma_start(ident[:, :], ident_d).then_inc(const_in, 16)
            g.dma_start(S["alibi"], alibi_d).then_inc(const_in, 16)
            g.dma_start(S["masks"], masks_d).then_inc(const_in, 16)
            for n in ("K0", "K1", "Q0", "Q1"):
                seq.mark(g.memset(flat(S[n]), 0.0))
            seq.wait()
            pool.wait_ge(hg_f, 4)
            g.tensor_scalar(flat(S["kk"]), flat(S["fT"]), -1.0, 1.0, ALU.mult, ALU.add).then_inc(hg_kk, 1)
            pool.wait_ge(hg_kk, 1)
            for i, b in enumerate(LEVELS):
                E = flat(S[f"D{i % 2}"]).rearrange("p (m two b) -> p m two b", two=2, b=b)
                kd = flat(S[f"K{i % 2}"]).rearrange("p (m two b) -> p m two b", two=2, b=b)
                qd = flat(S[f"Q{i % 2}"]).rearrange("p (m two b) -> p m two b", two=2, b=b)
                kk = flat(S["kk"]).rearrange("p (m two b) -> p m two b", two=2, b=b)
                qf = flat(S["qf"]).rearrange("p (m two b) -> p m two b", two=2, b=b)
                pool.wait_ge(hg_e, i + 1)
                if i == 0:
                    for g_ in (0, 1):
                        wait_unit_out(pool, g_)
                if i >= 2:
                    pool.wait_ge(hg_ps, i - 1)
                g.tensor_tensor(kd[:, :, 0, :], kk[:, :, 0, :], E[:, :, 0, :], ALU.mult).then_inc(hg_kq, 1)
                g.tensor_tensor(qd[:, :, 1, :], qf[:, :, 1, :], E[:, :, 1, :], ALU.mult).then_inc(hg_kq, 1)
            pool.wait_ge(h_new, H_MIX)
            g.dma_start(S["subk"], subk_d).then_inc(peer_in, 16)
            g.dma_start(S["iota"], iota_d).then_inc(peer_in, 16)

            for ph in range(4):
                tt, table = ph // 2, (u_d, v_d)[ph % 2]
                if ph % 2 == 0:
                    pool.wait_ge(idx_ready, tt + 1)
                n0 = ph * SLOTS
                with pool.Fori(0, SLOTS // 32) as it:
                    for hh in range(2):
                        pool.wait_ge(rows_used, it * 32 + (n0 + 16 * hh - 16 + PRIME))
                        pool.sem_inc(waited, 1)
                        g.tensor_copy(S["istage"][:, hh, :],
                                      S["idx"][:, tt, bass.ds(it * 32 + 16 * hh, 16)]).then_inc(staged, 1)
                        pool.wait_ge(staged, it * 2 + (ph * 8 + hh + 1))
                        pool.sem_inc(waited, 1)
                        for j in range(16):
                            n = n0 + 16 * hh + j
                            if j % 4 == 0:
                                pool.wait_ge(rows_used, it * 32 + (n + 4 - GRING + PRIME))
                                pool.sem_inc(waited, 1)
                            g.indirect_dma_start(S["rows"][:, n % GRING, :], None, table,
                                                 bass.IndirectOffsetOnAxis(S["istage"][:, hh, j:j + 1], 0)
                                                 ).then_inc(row_in[n % GRING], 16)
            pool.wait_ge(h_new, H_F)
            g.dma_start(S["rgw"], rg_d).then_inc(late_in, 16)
            seq.mark(g.memset(S["rxp"][:, :, 0:3], 0.0))
            seq.mark(g.memset(S["prod"][:, :, 0:2], 0.0))
            pool.wait_ge(rg_sig, 8)
            g.tensor_tensor(flat(S["ix"]), flat(S["iT"]), flat(S["xr"]), ALU.mult).then_inc(lru_ix, 1)
            pool.wait_ge(h_new, H_FFN0)
            g.dma_start(S["tri"], tri_d).then_inc(late_in, 16)
            g.dma_start(S["blk"], blk_d).then_inc(late_in, 16)
            g.dma_start(S["sbmask"], sbmask_d).then_inc(late_in, 16)
            pool.wait_ge(late_in, 64)
            for h in range(SBH):
                pool.wait_ge(z_w, h + 1)
                w = S[f"wz{h % 2}"].rearrange("p (c q) -> p c q", c=3)[:, 0:3:2, :]
                m = S["sbmask"][:, 1, :].rearrange("p (c q) -> p c q", c=3)[:, 0:3:2, :]
                g.tensor_tensor(w, w, m, ALU.mult).then_inc(z_wm, 1)

        @block.scalar
        def _(act):
            a = nc.scalar
            seq = Order(act, act_seq)

            def load_log_exp():
                a.preload_act_table_set("natural_log_exp_and_others")

            def norm(n, need_h, xn_free=None, shift=None):
                if n not in (0, 3):
                    load_log_exp()
                if need_h and shift is None:
                    act.wait_ge(h_new, need_h)
                for k in range(KT):
                    if shift is not None:
                        act.wait_ge(h_new, need_h - KT + k + 1)
                    a.activation(sq[:, k, :], hT[:, k, :], ACT.Square).then_inc(norm_sq, 1)
                act.wait_ge(norm_sum, n + 1)
                seq.mark(a.activation(lnv[:, :], NORM[:, 0:T], ACT.Ln, scale=1.0 / D, bias=col("eps")))
                seq.wait()
                a.activation(rstd[:, :], lnv[:, :], ACT.Exp, scale=-0.5).then_inc(norm_rs, 1)
                if shift is not None:
                    for k in range(KT):
                        act.wait_ge(norm_out, 8 * (n - 1) + k + 1)
                        if k == 0:
                            act.wait_ge(unit_done, xn_free)
                        a.activation(r32(xh[:, k, :]), sq[:, k, :], ACT.Identity, bias=shift[:, k:k + 1]
                                     ).then_inc(x_hi, 1)

            def split(g, it=0):
                act.wait_ge(landed[g % RING], it * 16 + 16 * (g // RING + 1))
                if g >= SPLIT0 + 2:
                    act.wait_ge(unit_done, it * 4 + (g - 1))
                a.activation(r32(S[f"whi{g % 2}"]), ring[:, g % RING, 0:2048], ACT.Copy).then_inc(w_hi, 1)

            def split_down(f, j, it=0):
                g = UNIT0[f"ffn{f}"] + j
                if j >= 2:
                    act.wait_ge(ffn_used, it * 4 + down_done(f, j - 2))
                a.activation(r32(S[f"dhi{j % 2}"]), ring[:, g % RING, 2048:3072], ACT.Copy).then_inc(d_hi, 1)

            def read_unit(g, fn, dst, **kw):
                act.wait_ge(unit_done, g + 1)
                a.activation(dst, bank[g % 2][:, :], fn, **kw).then_inc(unit_out[g % 2], 1)

            load_log_exp()
            act.wait_ge(x_in, 48)
            norm(0, 0)
            a.activation(silc[:, :], col("c", 0, 8), ACT.Silu).then_inc(silc_ready, 1)
            read_unit(0, ACT.Silu, flat(S["qf"][:, 0:2, :]))
            read_unit(1, ACT.Silu, flat(S["qf"][:, 2:4, :]))
            read_unit(2, ACT.Sigmoid, flat(S["fT"][:, 0:2, :]))
            read_unit(3, ACT.Sigmoid, flat(S["fT"][:, 2:4, :]))
            act.wait_ge(lam_a, 1)
            a.activation(small[:, 8:12], small[:, 4:8], ACT.Sigmoid).then_inc(lam_b, 1)
            load_log_exp()
            act.wait_ge(hg_f, 4)
            a.activation(flat(S["lf"]), flat(S["fT"]), ACT.Ln).then_inc(hg_lf, 1)

            def level_exp(i):
                act.wait_ge(hg_d, 2 * i + 2)
                a.activation(flat(S[f"D{i % 2}"]), flat(S[f"D{i % 2}"]), ACT.Exp).then_inc(hg_e, 1)

            def at_exp(i):
                nh = 2 if i < 4 else 4
                w = 512 // nh
                act.wait_ge(at_mx, i + 1)
                for h in range(nh):
                    a.activation(S[f"P{i % 2}"][:, h * w:(h + 1) * w], S[f"L{i % 2}"][:, h * w:(h + 1) * w],
                                 ACT.Exp, bias=S["osm"][:, 8 * (i % 2) + h:8 * (i % 2) + h + 1],
                                 accum_out=S["osm"][:, 16 + 8 * (i % 2) + h:17 + 8 * (i % 2) + h]).then_inc(at_p, 1)

            def at_copy(i):
                act.wait_ge(at_t, i + 1)
                if i >= 2:
                    act.wait_ge(at_o, i - 1)
                a.activation(flat(S[f"PT{i % 2}"]), bank[5][:, :], ACT.Copy).then_inc(at_pt, 1)

            for u in range(4, 14):
                if u in (4, 5):
                    read_unit(u, ACT.Copy, flat(S["qa"][:, 2 * (u - 4):2 * (u - 4) + 2, :]), scale=HD ** -0.5)
                if u in (12, 13):
                    c = u - 12
                    read_unit(u, ACT.Silu, S["grow"][:, :, 256 * c:256 * c + 256])
                i = u - 4
                if i < 8:
                    level_exp(i)
                if 0 <= u - 9 < 6:
                    at_exp(u - 9)
                if 0 <= u - 11 < 6:
                    at_copy(u - 11)
            at_exp(5)
            at_copy(3)
            at_copy(4)
            at_copy(5)
            for tt in range(TT):
                act.wait_ge(rec_o, tt + 1)
                if tt:
                    act.wait_ge(rec_var, 1)
                a.activation(flat(S["osq"]), bank[2 + tt][:, :], ACT.Square).then_inc(rec_ss, 1)
            act.wait_ge(rec_var, 2)
            seq.mark(a.activation(S["osm"][:, 40:48], S["osm"][:, 32:40], ACT.Ln, scale=1.0 / P, bias=col("eps")))
            seq.wait()
            a.activation(S["osm"][:, 48:56], S["osm"][:, 40:48], ACT.Exp, scale=-0.5).then_inc(rec_rs, 1)
            for tt in range(TT):
                act.wait_ge(rec_t, tt + 1)
                for h in range(RH):
                    a.activation(S["cat"][:, 4 + h, tt * P:(tt + 1) * P], bank[4 + tt][:, h * P:(h + 1) * P],
                                 ACT.Copy, scale=col("recg", h)).then_inc(rec_cat, 1)
            norm(1, H_MIX)
            for j in range(8):
                read_unit(UNIT0["peerq"] + j, ACT.Copy, flat(S["qpT"][:, 2 * j:2 * j + 2, :]))
            G0 = UNIT0["ada"]

            def ada_row(j, u, it):
                act.wait_ge(unit_done, it * 4 + (G0 + u + 1))
                if not isinstance(j, int) or j >= 2:
                    act.wait_ge(mcol_ps, it * 4 + (u - 1))
                a.activation(S["mrow"][0:1, u % 2, :], bank[(G0 + u) % 2][0:1, 0:ADA_COLS], ACT.Copy
                             ).then_inc(unit_out[(G0 + u) % 2], 1)
            for q in range(8):
                if q == 4:
                    for j in range(4):
                        ada_row(j, j, 0)
                act.wait_ge(sc_ps, q + 1)
                if q == 4:
                    act.wait_ge(sc_used, 1)
                a.activation(flat(S["s"][:, 4 * (q % 4):4 * (q % 4) + 4, :]), bank[[4, 5, 2, 3][q % 4]][:, :],
                             ACT.Copy).then_inc(sc_in, 1)
            looped(act, 4, 32, ada_row)
            for tt in range(TT):
                act.wait_ge(sc_sub, tt + 1)
                a.activation(S["gates"][:, tt, :], S["gates"][:, tt, :], ACT.Exp).then_inc(gate_e, 1)
            act.wait_ge(lam_a, 2)
            seq.mark(a.activation(small[:, 24:28], small[:, 20:24], ACT.Exp, scale=-1.0))
            seq.wait()
            a.activation(small[:, 28:32], small[:, 24:28], ACT.Ln, bias=col("one")).then_inc(lam_b, 1)
            for tt in range(TT):
                act.wait_ge(dots_kept, 8 * (tt + 1))
                if tt:
                    act.wait_ge(wts_ready, 1)
                a.activation(S["gel"], S["act"][:, tt, :], ACT.Gelu).then_inc(act_gelu, 1)
            norm(2, H_PEER)
            split(SPLIT0)
            split(SPLIT0 + 1)
            norm(3, H_F, UNIT0["ada"], shift=mcol[:, 0:8])
            G0 = UNIT0["l0in"]
            act.wait_ge(h_new, H_F)
            for j in range(2):
                act.wait_ge(unit_done, G0 + j + 1)
                a.activation(S["rxp"][:, 2 * j:2 * j + 2, 3:259],
                             bank[(G0 + j) % 2][:, :].rearrange("p (a t) -> p a t", a=2), ACT.Copy
                             ).then_inc(unit_out[(G0 + j) % 2], 1)
                split(G0 + j + 2)
            for j in (2, 3):
                read_unit(G0 + j, ACT.Gelu_apprx_tanh, flat(S["gg"][:, 2 * (j - 2):2 * (j - 2) + 2, :]))
                split(G0 + j + 2)
            for j in (4, 5):
                read_unit(G0 + j, ACT.Copy, flat(S["ac"][:, 2 * (j - 4):2 * (j - 4) + 2, :]))
                split(G0 + j + 2)
            for b in range(8):
                act.wait_ge(rg_ps, b // 2 + 1)
                dst = S["rT"] if b < 4 else S["iT"]
                a.activation(dst[:, b % 4, :], bank[2 + b // 2][:, 256 * (b % 2):256 * (b % 2) + 256], ACT.Sigmoid,
                             bias=col("ba" if b < 4 else "bx", b % 4)).then_inc(rg_sig, 1)
            split(G0 + 8)
            act.wait_ge(rg_sig, 4)
            for b in range(LH):
                a.activation(S["aT"][:, b, :], S["rT"][:, b, :], ACT.Exp, scale=small[:, 36 + b:37 + b]
                             ).then_inc(lru_t, 1)
            for b in range(LH):
                a.activation(S["tT"][:, b, :], S["rT"][:, b, :], ACT.Tanh, scale=small[:, 32 + b:33 + b]
                             ).then_inc(lru_t, 1)
            split(G0 + 9)
            load_log_exp()
            act.wait_ge(lru_c, 1)
            a.activation(flat(S["l1"]), flat(S["tT"]), ACT.Ln, scale=2.0).then_inc(lru_l, 1)
            a.activation(flat(S["l2"]), flat(S["tT"]), ACT.Ln, bias=col("one")).then_inc(lru_l, 1)
            split(G0 + 10)
            act.wait_ge(lru_d, 1)
            a.activation(flat(S["l1"]), flat(S["l1"]), ACT.Exp, scale=0.5).then_inc(lru_s, 1)
            split(G0 + 11)
            for half, src in enumerate((S["cv"], S["hs"])):
                if half == 0:
                    wait_unit_out(act, G0 + 8)
                    wait_unit_out(act, G0 + 9)
                else:
                    act.wait_ge(cat0_full, 1)
                a.activation(r32(flat(S["cat0h"][:, 4 * half:4 * half + 4, :])), flat(src), ACT.Copy
                             ).then_inc(cat0_hi, 1)
            for j in range(4):
                split(UNIT0["l0out"] + 2 + j)
                if j >= 2:
                    split_down(0, j - 2)
            norm(4, H_L0, UNIT0["ffn0"], shift=mcol[:, 24:32])

            def silu(f):
                G0 = UNIT0[f"ffn{f}"]

                n0 = FU * f

                def hidden(j, u, it):
                    act.wait_ge(unit_done, it * 4 + (G0 + u + 1))
                    if not isinstance(j, int) or j >= 2:
                        act.wait_ge(f_full, it * 4 + (n0 + u - 1))
                    a.activation(S[f"sg{u % 2}"], bank[(G0 + u) % 2][:, 0:256], ACT.Silu).then_inc(ffn_silu, 1)
                    act.wait_ge(f_full, it * 4 + (n0 + u + 1))
                    if not isinstance(j, int) or j >= 2:
                        act.wait_ge(ffn_used, it * 4 + down_done(f, u - 2))
                    a.activation(r32(S[f"fh{u % 2}"]), S[f"fa{u % 2}"], ACT.Copy).then_inc(f_hi, 1)

                def body(j, u, it):
                    hidden(j, u, it)
                    split(G0 + u + 2, it)
                    split_down(f, u + 2, it)
                body(0, 0, 0)
                body(1, 1, 0)
                looped(act, 2, FU - 4, body)
                for j in range(FU - 4, FU):
                    hidden(j, j, 0)
                    if j < FU - 2:
                        split(G0 + j + 2)
                        split_down(f, j + 2)
                    elif f == 0:
                        split(G0 + j + 2)
            silu(0)
            norm(5, H_FFN0, UNIT0["qkv"], shift=mcol[:, 48:56])
            G0 = UNIT0["qkv"]

            def qk_log(i):
                act.wait_ge(qk_sum, i + 1)
                a.activation(S["rsh"][:, i, :], bank[2 + i % 2][:, :], ACT.Ln, scale=1.0 / HD, bias=col("eps")
                             ).then_inc(qk_ln, 1)
            for i in range(8):
                dst = flat((S["qT"] if i < 4 else S["kT"])[:, 2 * (i % 4):2 * (i % 4) + 2, :])
                read_unit(G0 + i, ACT.Copy, dst)
                split(G0 + i + 2)
                wait_unit_out(act, G0 + i)
                if i >= 2:
                    act.wait_ge(qk_sum, i - 1)
                a.activation(S["sqh"][:, i % 2, :], dst, ACT.Square).then_inc(qk_sq, 1)
                if i:
                    qk_log(i - 1)
            qk_log(7)
            for c in range(4):
                read_unit(G0 + 8 + c, ACT.Copy, S["vrow"][:, :, 256 * c:256 * c + 256])
                split(G0 + 10 + c)
                for i in (2 * c, 2 * c + 1):
                    act.wait_ge(qk_ln, i + 1)
                    a.activation(S["rsh"][:, i, :], S["rsh"][:, i, :], ACT.Exp, scale=-0.5).then_inc(qk_rs, 1)

            def z_first(h):
                act.wait_ge(z_ps, h + 1)
                b = h % 2
                seq.mark(a.activation(S[f"az{b}"], bank[2 + b][:, 0:384], ACT.Abs))
                seq.wait()
                seq.mark(a.activation(S[f"ez{b}"], S[f"az{b}"], ACT.Exp, scale=-1.0))
                seq.wait()
                if h >= 2:
                    act.wait_ge(z_sp, h - 1)
                a.activation(S[f"lz{b}"], S[f"ez{b}"], ACT.Ln, bias=col("one")).then_inc(z_ln, 1)

            def z_second(h):
                act.wait_ge(z_arg, h + 1)
                if h >= 2:
                    act.wait_ge(z_o, h - 1)
                a.activation(S[f"wz{h % 2}"], S[f"ls{h % 2}"], ACT.Exp).then_inc(z_w, 1)

            def z_copy(pr):
                act.wait_ge(z_o, 2 * pr + 2)
                a.activation(r32(S["oTh"][:, pr, :]), bank[6 + pr % 2][:, 0:256], ACT.Copy).then_inc(z_out, 1)
            for h in range(SBH + 3):
                if h < SBH:
                    z_first(h)
                if 0 <= h - 1 < SBH:
                    z_second(h - 1)
                if h >= 3 and h % 2 == 1 and (h - 3) // 2 < 8:
                    z_copy((h - 3) // 2)
            for j in range(4):
                split(UNIT0["l1out"] + 2 + j)
                if j >= 2:
                    split_down(1, j - 2)
            norm(6, H_L1, UNIT0["ffn1"], shift=mcol[:, 72:80])
            silu(1)

        @block.vector
        def _(dve):
            v = nc.vector
            seq = Order(dve, dve_seq)

            def norm(n, gains, dst):
                dve.wait_ge(norm_rs, n + 1)
                for k in range(KT):
                    ins = v.scalar_tensor_tensor(dst[:, k, :], hT[:, k, :], gains[:, k:k + 1], rstd[:, :],
                                                 ALU.mult, ALU.mult)
                    ins.then_inc(h_new if dst is hT else norm_out, 1)

            def norm_split(n, gains, shift):
                dve.wait_ge(norm_sum, n + 1)
                norm(n, gains, sq)
                for k in range(KT):
                    dve.wait_ge(x_hi, 8 * (n - 3) + k + 1)
                    v.scalar_tensor_tensor(r32(xl[:, k, :]), sq[:, k, :], shift[:, k:k + 1], xh[:, k, :],
                                           ALU.add, ALU.subtract).then_inc(x_lo, 1)

            def split(g, it=0):
                dve.wait_ge(w_hi, it * 4 + (g - SPLIT0 + 1))
                v.tensor_tensor(r32(S[f"wlo{g % 2}"]), ring[:, g % RING, 0:2048], S[f"whi{g % 2}"],
                                ALU.subtract).then_inc(w_lo, 1)

            def split_down(f, j, it=0):
                g, n = UNIT0[f"ffn{f}"] + j, FU * f + j
                dve.wait_ge(d_hi, it * 4 + (n + 1))
                v.tensor_tensor(r32(S[f"dlo{j % 2}"]), ring[:, g % RING, 2048:3072], S[f"dhi{j % 2}"],
                                ALU.subtract).then_inc(d_lo, 1)

            def read_unit(g, dst):
                dve.wait_ge(unit_done, g + 1)
                v.tensor_copy(dst, bank[g % 2][:, :]).then_inc(unit_out[g % 2], 1)

            v.memset(small[:, 0:4], 0.0).then_inc(rows_used, PRIME)
            dve.wait_ge(x_in, 48)
            v.tensor_tensor(small[:, 4:8], col("lb", 0, 4), col("lb", 4, 4), ALU.subtract).then_inc(lam_a, 1)
            v.tensor_scalar(small[:, 16:20], col("lam", 0, 4), -1.0, None, ALU.mult).then_inc(dve_seq, 1)
            seq.n += 1
            seq.wait()
            v.tensor_tensor(small[:, 20:24], small[:, 16:20], col("lam", 0, 4), ALU.max).then_inc(lam_a, 1)
            norm(0, col("norm1", 0, 8), xn)
            dve.wait_ge(lam_b, 1)
            seq.mark(v.tensor_scalar(small[:, 12:16], small[:, 8:12], -1.0, 1.0, ALU.mult, ALU.add))
            seq.wait()
            wait_unit_out(dve, 2)
            wait_unit_out(dve, 3)
            for h in range(RH):
                v.tensor_scalar(S["fT"][:, h, :], S["fT"][:, h, :], small[:, 12 + h:13 + h], small[:, 8 + h:9 + h],
                                ALU.mult, ALU.add).then_inc(hg_f, 1)
            seq.mark(v.memset(flat(S["D1"]), 1.0))
            seq.wait()
            dve.wait_ge(hg_lf, 1)
            for h in range(RH):
                v.tensor_tensor_scan(S["cum"][:, h, :], S["D1"][:, h, :], S["lf"][:, h, :], 0.0, ALU.mult, ALU.add
                                     ).then_inc(hg_cum, 1)
            dve.wait_ge(hg_cum, 4)
            dve.wait_ge(const_in, 48)

            def level_diff(i):
                b = LEVELS[i]
                cum = flat(S["cum"]).rearrange("p (m two b) -> p m two b", two=2, b=b)
                Dd = flat(S[f"D{i % 2}"]).rearrange("p (m two b) -> p m two b", two=2, b=b)
                ref = cum[:, :, 0, b - 1:b].broadcast_to([P, T * RH // (2 * b), b])
                if i >= 2:
                    dve.wait_ge(hg_kq, 2 * (i - 1))
                v.tensor_tensor(Dd[:, :, 0, :], ref, cum[:, :, 0, :], ALU.subtract).then_inc(hg_d, 1)
                v.tensor_tensor(Dd[:, :, 1, :], cum[:, :, 1, :], ref, ALU.subtract).then_inc(hg_d, 1)

            def level_keep(i):
                dve.wait_ge(hg_ps, i + 1)
                if i == 0:
                    seq.mark(v.tensor_copy(flat(S["ST01"]), bank[2][:, :]))
                    v.memset(S["STd"].rearrange("p a b c -> p (a b c)"), 0.0).then_inc(hg_st, 1)
                    return
                mask = S["masks"][:, i - 1, :].unsqueeze(1).broadcast_to([P, 4, P])
                dve.wait_ge(hg_st, 2 * i - 1)
                for c in range(2):
                    o = S["STd"][:, 2 * c:2 * c + 2, :, :].rearrange("p a b t -> p (a b) t")
                    v.copy_predicated(o, mask, bank[2 + c][:, :].rearrange("p (a t) -> p a t", a=4)
                                      ).then_inc(hg_st, 1)

            def at_logits(i):
                dve.wait_ge(at_s, i + 1)
                if i >= 2:
                    dve.wait_ge(at_p, AT_P[i - 1])
                b = i % 2
                v.tensor_tensor(S[f"L{b}"], bank[4][:, :], S["alibi"][:, i, :], ALU.add).then_inc(at_l, 1)
                dve.wait_ge(at_l, i + 1)
                nh = 2 if i < 4 else 4
                m = S["osm"][:, 8 * b:8 * b + nh]
                if i >= 2:
                    dve.wait_ge(at_pn, AT_P[i - 1])
                seq.mark(v.tensor_reduce(m, S[f"L{b}"].rearrange("p (h k) -> p h k", h=nh), AX.X, ALU.max))
                seq.wait()
                v.tensor_scalar(m, m, -1.0, None, ALU.mult).then_inc(at_mx, 1)

            def at_norm(i):
                nh = 2 if i < 4 else 4
                w = 512 // nh
                b = i % 2
                dve.wait_ge(at_p, AT_P[i + 1])
                s = S["osm"][:, 16 + 8 * b:16 + 8 * b + nh]
                seq.mark(v.reciprocal(s, s))
                seq.wait()
                for h in range(nh):
                    p = S[f"P{b}"][:, h * w:(h + 1) * w]
                    v.tensor_scalar(p, p, s[:, h:h + 1], None, ALU.mult).then_inc(at_pn, 1)

            def at_store(i):
                dve.wait_ge(at_o, i + 1)
                p0 = 64 * (i % 2)
                if i < 4:
                    c = 2 * (i // 2)
                    v.tensor_copy(S["cat"][p0:p0 + 64, c:c + 2, P:T],
                                  bank[6][p0:p0 + 64, 0:T].rearrange("p (a t) -> p a t", a=2)).then_inc(at_cat, 1)
                else:
                    v.tensor_copy(S["cat"][p0:p0 + 64, 0:4, 0:P],
                                  bank[6][p0:p0 + 64, :].rearrange("p (a t) -> p a t", a=4)).then_inc(at_cat, 1)

            AT_P = [0, 2, 4, 6, 8, 12, 16]
            level_diff(0)
            for u in range(4, 14):
                if u in (6, 7):
                    read_unit(u, flat(S["ka"][:, 2 * (u - 6):2 * (u - 6) + 2, :]))
                if u in (8, 9, 10, 11):
                    c = u % 2
                    dst = S["va"] if u < 10 else S["irow"]
                    dve.wait_ge(unit_done, u + 1)
                    v.tensor_copy(dst[:, :, 256 * c:256 * c + 256],
                                  bank[u % 2][:, :].rearrange("p (a n) -> p a n", a=2)).then_inc(unit_out[u % 2], 1)
                if 0 <= u - 12 < 6:
                    at_store(u - 12)
                i = u - 4
                if i < 7:
                    level_diff(i + 1)
                if i < 8:
                    level_keep(i)
                if i == 8:
                    dve.wait_ge(hg_ps, 9)
                    dve.wait_ge(hg_st, 15)
                    for c in range(2):
                        o = S["STd"][:, 2 * c:2 * c + 2, :, :].rearrange("p a b t -> p (a b) t")
                        m = ident[:, :].bitcast(I32).unsqueeze(1).broadcast_to([P, 4, P])
                        v.copy_predicated(o, m, bank[2 + c][:, :].rearrange("p (a t) -> p a t", a=4)
                                          ).then_inc(hg_st, 1)
                if 0 <= u - 8 < 6:
                    at_logits(u - 8)
                if 0 <= u - 9 < 6:
                    at_norm(u - 9)
            at_norm(5)
            for i in (2, 3, 4, 5):
                at_store(i)
            for tt in range(TT):
                dve.wait_ge(rec_ss, tt + 1)
                v.tensor_reduce(S["osm"][:, 32 + 4 * tt:36 + 4 * tt], S["osq"], AX.X, ALU.add).then_inc(rec_var, 1)
            dve.wait_ge(rec_rs, 1)
            wait_unit_out(dve, 12)
            wait_unit_out(dve, 13)
            for tt in range(TT):
                o = S[f"orow{tt}"]
                r = S["osm"][:, 48 + 4 * tt:52 + 4 * tt].unsqueeze(2).broadcast_to([P, RH, P])
                seq.mark(v.tensor_tensor(o, bank[2 + tt][:, :].rearrange("p (h e) -> p h e", h=RH), r, ALU.mult))
                seq.wait()
                v.tensor_tensor(flat(o), flat(o), S["grow"][:, tt, :], ALU.mult).then_inc(rec_row, 1)
            for j in range(4):
                g = UNIT0["outproj"] + j
                dve.wait_ge(unit_done, g + 1)
                h2 = flat(hT[:, 2 * j:2 * j + 2, :])
                v.tensor_tensor(h2, bank[g % 2][:, :], h2, ALU.add).then_inc(h_new, 1)
            norm(1, col("norm2", 0, 8), xn)
            for q in range(4):
                tt, b = q // 2, [2, 3, 6, 7][q]
                dve.wait_ge(hn_t, q + 1)
                v.tensor_copy(S["hnrow"][:, tt, 512 * (q % 2):512 * (q % 2) + 512], bank[b][:, :]
                              ).then_inc(hn_row, 1)

            def top16(vals, work, top, pos, n):
                for i in range(n):
                    last = v.max(top[:, i, 0:8], vals[:, i, :])
                seq.mark(last)
                seq.wait()
                for i in range(n):
                    last = v.match_replace(work[:, i, :], top[:, i, 0:8], vals[:, i, :], -3.0e38)
                    v.max_index(pos[:, i, 0:8], top[:, i, 0:8], vals[:, i, :]) if i < n - 1 else None
                seq.mark(v.max_index(pos[:, n - 1, 0:8], top[:, n - 1, 0:8], vals[:, n - 1, :]))
                seq.wait()
                for i in range(n):
                    last = v.max(top[:, i, 8:16], work[:, i, :])
                seq.mark(last)
                seq.wait()
                for i in range(n):
                    last = v.max_index(pos[:, i, 8:16], top[:, i, 8:16], work[:, i, :])
                return last

            dve.wait_ge(peer_in, 32)
            for tt in range(TT):
                dve.wait_ge(sc_in, 4 * tt + 4)
                v16, i16 = S["v16"], S["i16"]
                top16(S["s"], S["s2"], v16, i16, 16).then_inc(sc_used, 1)
                dve.wait_ge(sc_used, tt + 1)
                seq.mark(v.tensor_copy(flat(S["if16"]), flat(i16)))
                a4 = v16.rearrange("p (h c) i -> p h c i", c=2)
                in0 = a4[:, :, 0, :].unsqueeze(3).broadcast_to([P, PH, 16, 16])
                in1 = a4[:, :, 1, :].unsqueeze(2).broadcast_to([P, PH, 16, 16])
                seq.mark(v.tensor_tensor(S["cand"].rearrange("p h (i j) -> p h i j", i=16), in0, in1, ALU.add))
                seq.wait()
                seq.mark(top16(S["cand"], S["cand2"], S["sc"], S["pos"], PH))
                seq.wait()
                seq.mark(v.tensor_scalar(S["posa"], flat(S["pos"]), 4, None, ALU.logical_shift_right))
                seq.mark(v.tensor_scalar(S["posb"], flat(S["pos"]), 15, None, ALU.bitwise_and))
                seq.wait()
                seq.mark(v.tensor_copy(S["fa"], S["posa"]))
                seq.mark(v.tensor_copy(S["fb"], S["posb"]))
                seq.wait()
                f4 = S["if16"].rearrange("p (h c) i -> p h c i", c=2)
                oh = S["oh"]
                for c, (f, e) in enumerate(((S["fa"], S["e1"]), (S["fb"], S["e2"]))):
                    seq.mark(v.tensor_tensor(oh, f.unsqueeze(2).broadcast_to([P, SLOTS, 16]),
                                             S["iota"].unsqueeze(1).broadcast_to([P, SLOTS, 16]), ALU.is_equal))
                    seq.wait()
                    oh4 = oh.rearrange("p (h k) i -> p h k i", h=PH)
                    seq.mark(v.tensor_tensor(oh4, oh4, f4[:, :, c, :].unsqueeze(2).broadcast_to([P, PH, 16, 16]),
                                             ALU.mult))
                    seq.wait()
                    seq.mark(v.tensor_reduce(e, oh, AX.X, ALU.add))
                    seq.wait()
                seq.mark(v.scalar_tensor_tensor(S["e1"], S["e1"], float(NK), S["e2"], ALU.mult, ALU.add))
                seq.wait()
                v.tensor_copy(S["idx"][:, tt, :], S["e1"]).then_inc(idx_ready, 1)
                g3 = S["gates"][:, tt, :].rearrange("p (h k) -> p h k", h=PH)
                v.tensor_tensor(g3, S["sc"], S["sc"][:, :, 0:1].broadcast_to([P, PH, 16]), ALU.subtract
                                ).then_inc(sc_sub, 1)
            for i in range(4):
                seq.mark(v.memset(S["acc"][:, i, :], 0.0))
            seq.wait()
            for ph in range(4):
                tt, n0 = ph // 2, ph * SLOTS
                if ph % 2 == 0:
                    dve.wait_ge(hn_row, 4)
                    with dve.Fori(0, SLOTS // 16) as it:
                        for j in range(16):
                            n = n0 + j
                            dve.wait_ge(row_in[n % GRING], it * 32 + 16 * (n // GRING + 1))
                            dve.wait_ge(rows_used, it * 16 + (n - 1 + PRIME))
                            v.tensor_tensor_reduce(S["junk"][:, j % 2, :], S["rows"][:, n % GRING, :],
                                                   S["hnrow"][:, tt, :], 1.0, 0.0, ALU.mult, ALU.add,
                                                   S["astage"][:, 0, j:j + 1]).then_inc(rows_used, 1)
                        dve.wait_ge(rows_used, it * 16 + (n0 + 16 + PRIME))
                        v.tensor_copy(S["act"][:, tt, bass.ds(it * 16, 16)], S["astage"][:, 0, :]
                                      ).then_inc(dots_kept, 1)
                        dve.wait_ge(dots_kept, it + (8 * tt + 1))
                    g3 = S["gates"][:, tt, :].rearrange("p (h k) -> p h k", h=PH)
                    dve.wait_ge(gate_e, tt + 1)
                    t8 = S["tiny"][:, 8 * tt:8 * tt + 8]
                    seq.mark(v.tensor_reduce(t8, g3, AX.X, ALU.add))
                    seq.wait()
                    seq.mark(v.reciprocal(t8, t8))
                    seq.wait()
                    seq.mark(v.tensor_tensor(g3, g3, t8.unsqueeze(2).broadcast_to([P, PH, 16]), ALU.mult))
                    seq.wait()
                    dve.wait_ge(act_gelu, tt + 1)
                    v.tensor_tensor(S["wts"][:, tt, :], S["gel"], S["gates"][:, tt, :], ALU.mult
                                    ).then_inc(wts_ready, 1)
                    dve.wait_ge(wts_ready, tt + 1)
                else:
                    with dve.Fori(0, SLOTS // 16) as it:
                        for j in range(16):
                            n = n0 + j
                            dve.wait_ge(row_in[n % GRING], it * 32 + 16 * (n // GRING + 1))
                            dve.wait_ge(rows_used, it * 16 + (n - 1 + PRIME))
                            acc = S["acc"][:, 2 * tt + j % 2, :]
                            v.scalar_tensor_tensor(acc, S["rows"][:, n % GRING, :],
                                                   S["wts"][:, tt, bass.ds(it * 16 + j, 1)], acc,
                                                   ALU.mult, ALU.add).then_inc(rows_used, 1)
                    dve.wait_ge(rows_used, n0 + SLOTS + PRIME)
                    v.tensor_tensor(S["acc"][:, 2 * tt, :], S["acc"][:, 2 * tt, :], S["acc"][:, 2 * tt + 1, :],
                                    ALU.add).then_inc(acc_ready, 1)
            dve.wait_ge(lam_b, 2)
            seq.mark(v.scalar_tensor_tensor(small[:, 40:44], small[:, 16:20], 0.0, small[:, 28:32], ALU.max, ALU.add))
            seq.wait()
            seq.mark(v.tensor_scalar(small[:, 32:36], small[:, 40:44], 8.0, None, ALU.mult))
            seq.mark(v.tensor_scalar(small[:, 36:40], small[:, 40:44], -8.0, None, ALU.mult))
            seq.mark(v.tensor_scalar(small[:, 44:45], col("qn"), HD ** -0.5, None, ALU.mult))
            dve.wait_ge(mcol_ps, 32)
            seq.mark(v.tensor_tensor(mcol[:, :], bank[6][:, 0:96], col("adab", 0, 96), ALU.add))
            seq.wait()
            for i, (n, c) in enumerate((("mix0", 8), ("ffng0", 32), ("mix1", 56), ("ffng1", 80))):
                v.scalar_tensor_tensor(gain[:, i, :], mcol[:, c:c + 8], 1.0, col(n, 0, 8), ALU.add, ALU.mult
                                       ).then_inc(mcol_ready, 1)
            for q in range(4):
                tt, half = q // 2, q % 2
                dve.wait_ge(po_t, q + 1)
                h4 = hT[:, 4 * half:4 * half + 4, tt * P:(tt + 1) * P]
                v.tensor_tensor(h4, bank[2 + q][:, :].rearrange("p (k t) -> p k t", k=4), h4, ALU.add
                                ).then_inc(h_new, 1)
            dve.wait_ge(h_new, H_PEER)
            norm(2, col("normf", 0, 8), hT)
            split(SPLIT0)
            split(SPLIT0 + 1)
            dve.wait_ge(h_new, H_F)
            dve.wait_ge(mcol_ready, 4)
            norm_split(3, gain[:, 0, :], mcol[:, 0:8])
            G0 = UNIT0["l0in"]
            dve.wait_ge(pool_seq, 6)
            for j in (2, 3):
                split(G0 + j)
            wait_unit_out(dve, G0)
            wait_unit_out(dve, G0 + 1)
            for k in range(4):
                for b in range(LH):
                    src = S["rxp"][:, b, k:k + T]
                    w = col("wb", 4 * k + b)
                    if k == 0:
                        ins = v.tensor_scalar(S["xr"][:, b, :], src, w, col("bb", b), ALU.mult, ALU.add)
                    else:
                        ins = v.scalar_tensor_tensor(S["xr"][:, b, :], src, w, S["xr"][:, b, :], ALU.mult, ALU.add)
                    if k == 3:
                        ins.then_inc(xr_ready, 1)
                    else:
                        seq.mark(ins)
                if k < 3:
                    seq.wait()
                if k in (0, 2):
                    split(G0 + 4 + k // 2)
            for j in (6, 7):
                split(G0 + j)
            for j in (6, 7):
                dve.wait_ge(unit_done, G0 + j + 1)
                wait_unit_out(dve, G0 + j - 2)
                c = 2 * (j - 6)
                v.tensor_tensor(S["prod"][:, c:c + 2, 2:258],
                                bank[(G0 + j) % 2][:, :].rearrange("p (a t) -> p a t", a=2),
                                S["ac"][:, c:c + 2, :], ALU.mult).then_inc(unit_out[(G0 + j) % 2], 1)
                split(G0 + j + 2)
            dve.wait_ge(lru_t, 8)
            v.tensor_scalar(flat(S["tT"]), flat(S["tT"]), 1e-18, None, ALU.max).then_inc(lru_c, 1)
            wait_unit_out(dve, G0 + 6)
            wait_unit_out(dve, G0 + 7)
            for k in range(3):
                for b in range(4):
                    src = S["prod"][:, b, k:k + T]
                    w = col("wa", 4 * k + b)
                    if k == 0:
                        ins = v.tensor_scalar(S["cv"][:, b, :], src, w, None, ALU.mult)
                    else:
                        ins = v.scalar_tensor_tensor(S["cv"][:, b, :], src, w, S["cv"][:, b, :], ALU.mult, ALU.add)
                    seq.mark(ins)
                seq.wait()
            dve.wait_ge(lru_l, 2)
            v.tensor_tensor(flat(S["l1"]), flat(S["l1"]), flat(S["l2"]), ALU.subtract).then_inc(lru_d, 1)
            for j in (8, 9):
                dve.wait_ge(unit_done, G0 + j + 1)
                c = 2 * (j - 8)
                v.tensor_tensor(flat(S["cv"][:, c:c + 2, :]), bank[(G0 + j) % 2][:, :],
                                flat(S["cv"][:, c:c + 2, :]), ALU.mult).then_inc(unit_out[(G0 + j) % 2], 1)
            split(G0 + 10)
            dve.wait_ge(lru_s, 1)
            dve.wait_ge(lru_ix, 1)
            seq.mark(v.tensor_tensor(flat(S["bT"]), flat(S["l1"]), flat(S["ix"]), ALU.mult))
            seq.wait()
            for b in range(LH):
                seq.mark(v.tensor_tensor_scan(S["hs"][:, b, :], S["aT"][:, b, :], S["bT"][:, b, :], 0.0,
                                              ALU.mult, ALU.add))
            seq.wait()
            v.tensor_tensor(flat(S["hs"]), flat(S["hs"]), flat(S["gg"]), ALU.mult).then_inc(cat0_full, 1)
            split(G0 + 11)
            for half, src in enumerate((S["cv"], S["hs"])):
                dve.wait_ge(cat0_hi, half + 1)
                v.tensor_tensor(r32(flat(S["cat0l"][:, 4 * half:4 * half + 4, :])), flat(src),
                                flat(S["cat0h"][:, 4 * half:4 * half + 4, :]), ALU.subtract).then_inc(cat0_ready, 1)

            def gated_residual(name, m0, f):
                for j in range(4):
                    split(UNIT0[name] + j + 2)
                    if j >= 2:
                        split_down(f, j - 2)
                    g = UNIT0[name] + j
                    dve.wait_ge(unit_done, g + 1)
                    for k in (2 * j, 2 * j + 1):
                        ins = v.scalar_tensor_tensor(hT[:, k, :], bank[g % 2][:, 256 * (k % 2):256 * (k % 2) + 256],
                                                     mcol[:, m0 + k:m0 + k + 1], hT[:, k, :], ALU.mult, ALU.add)
                        ins.then_inc(h_new, 1)

            def swiglu(f, m0):
                G0 = UNIT0[f"ffn{f}"]

                def hidden(j, u, it):
                    fa, fh, fl = (S[f"{n}{u % 2}"] for n in ("fa", "fh", "fl"))
                    dve.wait_ge(ffn_silu, it * 4 + (FU * f + u + 1))
                    if not isinstance(j, int) or j >= 2:
                        dve.wait_ge(f_lo, it * 4 + (FU * f + u - 1))
                    v.tensor_tensor(fa, S[f"sg{u % 2}"], bank[(G0 + u) % 2][:, 256:512], ALU.mult
                                    ).then_inc(f_full, 1)
                    dve.wait_ge(f_hi, it * 4 + (FU * f + u + 1))
                    v.tensor_tensor(r32(fl), fa, fh, ALU.subtract).then_inc(f_lo, 1)

                def body(j, u, it):
                    hidden(j, u, it)
                    split(G0 + u + 2, it)
                    split_down(f, u + 2, it)
                body(0, 0, 0)
                body(1, 1, 0)
                looped(dve, 2, FU - 4, body)
                for j in range(FU - 4, FU):
                    hidden(j, j, 0)
                    if j < FU - 2:
                        split(G0 + j + 2)
                        split_down(f, j + 2)
                    elif f == 0:
                        split(G0 + j + 2)
                for k in range(KT):
                    dve.wait_ge(bank_full, 4 * f + k // 2 + 1)
                    v.scalar_tensor_tensor(hT[:, k, :], bank[2 + k // 2][:, 256 * (k % 2):256 * (k % 2) + 256],
                                           mcol[:, m0 + k:m0 + k + 1], hT[:, k, :], ALU.mult, ALU.add
                                           ).then_inc(h_new, 1)
            gated_residual("l0out", 16, 0)
            dve.wait_ge(h_new, H_L0)
            norm_split(4, gain[:, 1, :], mcol[:, 24:32])
            swiglu(0, 40)
            dve.wait_ge(h_new, H_FFN0)
            norm_split(5, gain[:, 2, :], mcol[:, 48:56])
            G0 = UNIT0["qkv"]
            for i in range(10):
                split(G0 + 2 + i)
            for i in range(8):
                dst = flat((S["qT"] if i < 4 else S["kT"])[:, 2 * (i % 4):2 * (i % 4) + 2, :])
                dve.wait_ge(qk_rs, i + 1)
                v.scalar_tensor_tensor(dst, dst, small[:, 44:45] if i < 4 else col("kn"), S["rsh"][:, i, :],
                                       ALU.mult, ALU.mult).then_inc(qk_ready, 1)
            split(G0 + 12)
            split(G0 + 13)
            dve.wait_ge(late_in, 64)

            def z_first(h):
                b = h % 2
                z = bank[2 + b][:, 0:384]
                dve.wait_ge(z_ln, h + 1)
                v.scalar_tensor_tensor(S[f"sp{b}"], z, 0.0, S[f"lz{b}"], ALU.max, ALU.add).then_inc(z_sp, 1)
                dve.wait_ge(z_sp, h + 1)
                if h >= 2:
                    dve.wait_ge(z_af, h - 1)
                    dve.wait_ge(z_w, h - 1)
                v.tensor_tensor(S[f"lk{b}"], S[f"sp{b}"], S["sbmask"][:, 0, :], ALU.mult).then_inc(z_lk, 1)
                v.scalar_tensor_tensor(S[f"ls{b}"], z, 1.0, S[f"sp{b}"], ALU.mult, ALU.subtract).then_inc(z_ls, 1)

            def z_second(h):
                b = h % 2
                dve.wait_ge(z_af, h + 1)
                dve.wait_ge(z_ls, h + 1)
                v.tensor_tensor(S[f"ls{b}"], S[f"ls{b}"], bank[4 + b][:, 0:384], ALU.add).then_inc(z_arg, 1)
            def z_low(pr):
                dve.wait_ge(z_out, pr + 1)
                v.tensor_tensor(r32(S["oTl"][:, pr, :]), bank[6 + pr % 2][:, 0:256], S["oTh"][:, pr, :],
                                ALU.subtract).then_inc(z_lo, 1)
            for h in range(SBH + 4):
                if 1 <= h <= SBH:
                    z_second(h - 1)
                if h < SBH:
                    z_first(h)
                if h >= 4 and h % 2 == 0 and (h - 4) // 2 < 8:
                    z_low((h - 4) // 2)
            gated_residual("l1out", 64, 1)
            dve.wait_ge(h_new, H_L1)
            norm_split(6, gain[:, 3, :], mcol[:, 72:80])
            swiglu(1, 88)

        @block.tensor
        def _(pe):
            t = nc.tensor

            def norm(n):
                for k in range(KT):
                    pe.wait_ge(norm_sq, 8 * n + k + 1)
                    ins = t.matmul(NORM[:, 0:T], ones[:, :], sq[:, k, :], start=(k == 0), stop=(k == KT - 1))
                ins.then_inc(norm_sum, 1)

            def unit_start(g, it=0, regs=False):
                pe.wait_ge(landed[g % RING], it * 16 + 16 * (g // RING + 1))
                if g >= 2:
                    wait_unit_out(pe, g - 2, it)

            def features(g, src, ready=None):
                w = ring[:, g % RING, 0:2048].rearrange("p (b k c) -> p b k c", b=2, k=KT)
                for b in range(2):
                    for k in range(KT):
                        if ready is not None and b == 0:
                            pe.wait_ge(ready[0], ready[1] + k + 1)
                        ins = t.matmul(bank[g % 2][:, b * T:(b + 1) * T], w[:, b, k, :], src[:, k, :],
                                       start=(k == 0), stop=(k == KT - 1))
                ins.then_inc(unit_done, 1)

            def rows(g, src):
                w = ring[:, g % RING, 0:2048].rearrange("p (b k c) -> p b k c", b=2, k=KT)
                for tt in range(TT):
                    for k in range(KT):
                        ins = t.matmul(bank[g % 2][:, tt * 256:tt * 256 + 256].rearrange("p (b c) -> p b c", b=2),
                                       src[:, k, tt * P:(tt + 1) * P], w[:, :, k, :],
                                       start=(k == 0), stop=(k == KT - 1))
                ins.then_inc(unit_done, 1)

            THREE = ((0, 0), (0, 1), (1, 0))

            def split_features(g, hi, lo, ready=None):
                pe.wait_ge(w_lo, g - SPLIT0 + 1)
                wait_unit_out(pe, g - 2)
                w = [S[f"{n}{g % 2}"].rearrange("p (b k c) -> p b k c", b=2, k=KT) for n in ("whi", "wlo")]
                for b in range(2):
                    for k in range(KT):
                        if ready is not None and b == 0:
                            pe.wait_ge(x_lo, ready + k + 1)
                        for i, j in THREE:
                            ins = t.matmul(bank[g % 2][:, b * T:(b + 1) * T], r32(w[i][:, b, k, :]),
                                           r32((hi, lo)[j][:, k, :]), start=(k == 0 and i + j == 0),
                                           stop=(k == KT - 1 and i == 1))
                ins.then_inc(unit_done, 1)

            def split_rows(g, hi, lo):
                pe.wait_ge(w_lo, g - SPLIT0 + 1)
                wait_unit_out(pe, g - 2)
                w = [S[f"{n}{g % 2}"].rearrange("p (b k c) -> p b k c", b=2, k=KT) for n in ("whi", "wlo")]
                for tt in range(TT):
                    for k in range(KT):
                        for i, j in THREE:
                            ins = t.matmul(bank[g % 2][:, tt * 256:tt * 256 + 256].rearrange("p (b c) -> p b c", b=2),
                                           r32((hi, lo)[j][:, k, tt * P:(tt + 1) * P]), r32(w[i][:, :, k, :]),
                                           start=(k == 0 and i + j == 0), stop=(k == KT - 1 and i == 1))
                ins.then_inc(unit_done, 1)

            pe.wait_ge(x_in, 48)
            norm(0)

            def level(i):
                if i < 8:
                    pe.wait_ge(hg_kq, 2 * i + 2)
                if i > 0:
                    pe.wait_ge(hg_st, 2 * i - 1)
                if i < 8:
                    kd, qd = S[f"K{i % 2}"], S[f"Q{i % 2}"]
                else:
                    kd, qd = S["kk"], S["qf"]
                for h in range(RH):
                    if i == 0:
                        ins = t.matmul(bank[2][:, h * P:(h + 1) * P], kd[:, h, 0:P], qd[:, h, P:T],
                                       start=True, stop=True)
                        continue
                    for tt in range(TT):
                        at = (2 * (h % 2) + tt) * P
                        ins = t.matmul(bank[2 + h // 2][:, at:at + P], kd[:, h, tt * P:(tt + 1) * P],
                                       qd[:, h, tt * P:(tt + 1) * P], start=True, stop=True)
                ins.then_inc(hg_ps, 1)

            def at_scores(i):
                if i == 0:
                    for g in (4, 5, 6, 7):
                        wait_unit_out(pe, g)
                else:
                    pe.wait_ge(at_l, i)
                for c in range(2 if i < 4 else 4):
                    h = at_head(i, c)
                    p0 = 64 * (h % 2)
                    n = T if i < 4 else P
                    q0 = P if i < 4 else 0
                    ins = t.matmul(bank[4][:, c * n:(c + 1) * n], S["qa"][p0:p0 + 64, h // 2, q0:q0 + P],
                                   S["ka"][p0:p0 + 64, h // 2, 0:n], start=True, stop=True)
                ins.then_inc(at_s, 1)

            AT_P = [0, 2, 4, 6, 8, 12, 16]

            def at_transpose(i):
                pe.wait_ge(at_pn, AT_P[i + 1])
                if i:
                    pe.wait_ge(at_pt, i)
                for c in range(4):
                    ins = t.transpose(bank[5][:, c * P:(c + 1) * P], S[f"P{i % 2}"][:, c * P:(c + 1) * P],
                                      ident[:, :])
                ins.then_inc(at_t, 1)

            def at_out(i):
                pe.wait_ge(at_pt, i + 1)
                if i == 0:
                    wait_unit_out(pe, 8)
                    wait_unit_out(pe, 9)
                else:
                    pe.wait_ge(at_cat, i)
                pt = S[f"PT{i % 2}"]
                p0 = 64 * (i % 2)
                for c in range(2 if i < 4 else 4):
                    h = at_head(i, c)
                    for kt in range(2 if i < 4 else 1):
                        ins = t.matmul(bank[6][p0:p0 + 64, c * P:(c + 1) * P], S["va"][:, kt, h * HD:(h + 1) * HD],
                                       pt[:, 2 * c + kt if i < 4 else c, :], start=(kt == 0), stop=(i >= 4 or kt == 1))
                ins.then_inc(at_o, 1)

            for u in range(14):
                unit_start(u)
                if u < 8:
                    features(u, xn, (norm_out, 0) if u == 0 else None)
                else:
                    rows(u, xn)
                if u >= 4 and u - 4 < 9:
                    level(u - 4)
                if u == 10:
                    pe.wait_ge(const_in, 48)
                if 0 <= u - 10 < 6:
                    at_transpose(u - 10)
                if 0 <= u - 8 < 6:
                    at_scores(u - 8)
                if 0 <= u - 11 < 6:
                    at_out(u - 11)
            at_transpose(4)
            at_out(3)
            at_transpose(5)
            at_out(4)
            pe.wait_ge(hg_st, 17)
            wait_unit_out(pe, 10)
            wait_unit_out(pe, 11)
            for tt in range(TT):
                for h in range(RH):
                    o = bank[2 + tt][:, h * P:(h + 1) * P]
                    if tt:
                        t.matmul(o, S["ST01"][:, h, :], S["irow"][:, 0, h * P:(h + 1) * P], start=True, stop=False)
                    ins = t.matmul(o, S["STd"][:, h, tt, :], S["irow"][:, tt, h * P:(h + 1) * P],
                                   start=(tt == 0), stop=True)
                ins.then_inc(rec_o, 1)
            at_out(5)
            for tt in range(TT):
                pe.wait_ge(rec_row, tt + 1)
                if tt == 0:
                    pe.wait_ge(at_l, 6)
                else:
                    pe.wait_ge(at_pt, 6)
                for h in range(RH):
                    ins = t.transpose(bank[4 + tt][:, h * P:(h + 1) * P], S[f"orow{tt}"][:, h, :], ident[:, :])
                ins.then_inc(rec_t, 1)
            pe.wait_ge(at_cat, 6)
            pe.wait_ge(rec_cat, 8)
            for j in range(4):
                g = UNIT0["outproj"] + j
                unit_start(g)
                features(g, S["cat"])
            norm(1)
            for j in range(8):
                g = UNIT0["peerq"] + j
                unit_start(g)
                features(g, xn, (norm_out, 8) if j == 0 else None)
            for q in range(4):
                tt, b = q // 2, [2, 3, 6, 7][q]
                for k in range(4):
                    ins = t.transpose(bank[b][:, k * P:(k + 1) * P],
                                      xn[:, 4 * (q % 2) + k, tt * P:(tt + 1) * P], ident[:, :])
                ins.then_inc(hn_t, 1)
            wait_unit_out(pe, UNIT0["peerq"] + 6)
            wait_unit_out(pe, UNIT0["peerq"] + 7)
            pe.wait_ge(peer_in, 32)
            pe.wait_ge(hn_row, 2)
            for q in range(8):
                tt = q // 4
                if q >= 4:
                    pe.wait_ge(sc_in, q - 3)
                for c in range(4):
                    hc = 4 * (q % 4) + c
                    ins = t.matmul(bank[[4, 5, 2, 3][q % 4]][:, c * P:(c + 1) * P],
                                   S["qpT"][:, hc, tt * P:(tt + 1) * P], S["subk"][:, hc, :], start=True, stop=True)
                ins.then_inc(sc_ps, 1)
            pe.wait_ge(silc_ready, 1)
            pe.wait_ge(hn_row, 4)
            G0 = UNIT0["ada"]

            def ada_unit(j, u, it):
                g = G0 + u
                pe.wait_ge(landed[g % RING], it * 16 + 16 * (g // RING + 1))
                wait_unit_out(pe, g - 2, it)
                w = ring[:, g % RING, :].rearrange("p (k c) -> p k c", k=KT)
                for k in range(KT):
                    ins = t.matmul(bank[g % 2][0:1, 0:ADA_COLS], silc[:, k:k + 1], w[:, k, :],
                                   start=(k == 0), stop=(k == KT - 1))
                ins.then_inc(unit_done, 1)

            def ada_column(j, u, it):
                wait_unit_out(pe, G0 + u, it)
                for c in range(3):
                    at = j * 3 + c
                    o = bank[6][:, at:at + 1] if isinstance(at, int) else bank[6][:, bass.ds(at, 1)]
                    ins = t.matmul(o, S["mrow"][0:1, u % 2, c * P:(c + 1) * P], ones[0:1, 0:1], start=True, stop=True)
                ins.then_inc(mcol_ps, 1)
            ada_unit(0, 0, 0)

            def both(j, u, it):
                ada_unit(j, u, it)
                ada_column(j - 1, u - 1, it)
            looped(pe, 1, 32, both)
            ada_column(31, 31, 0)
            for q in range(4):
                tt, half = q // 2, q % 2
                pe.wait_ge(acc_ready, tt + 1)
                for k in range(4):
                    at = (4 * half + k) * P
                    ins = t.transpose(bank[2 + q][:, k * P:(k + 1) * P], S["acc"][:, 2 * tt, at:at + P], ident[:, :])
                ins.then_inc(po_t, 1)
            norm(2)
            norm(3)
            G0 = UNIT0["l0in"]
            for j in range(10):
                split_features(G0 + j, xh, xl, 0 if j == 0 else None)
                if j == 4:
                    pe.wait_ge(late_in, 16)
                    pe.wait_ge(xr_ready, 4)
                    for b in range(8):
                        ins = t.matmul(bank[2 + b // 2][:, 256 * (b % 2):256 * (b % 2) + 256], S["rgw"][:, b, :],
                                       S["xr"][:, b % 4, :], start=True, stop=True)
                        if b % 2:
                            ins.then_inc(rg_ps, 1)
            wait_unit_out(pe, G0 + 8)
            wait_unit_out(pe, G0 + 9)
            pe.wait_ge(cat0_ready, 2)
            for j in range(4):
                split_features(UNIT0["l0out"] + j, S["cat0h"], S["cat0l"])
            norm(4)

            def swiglu(f):
                G0 = UNIT0[f"ffn{f}"]

                def gate_up(j, u, it):
                    g = G0 + u
                    pe.wait_ge(w_lo, it * 4 + (g - SPLIT0 + 1))
                    if isinstance(j, int) and j < 2:
                        wait_unit_out(pe, g - 2)
                    else:
                        pe.wait_ge(f_full, it * 4 + (FU * f + u - 1))
                    w = [S[f"{n}{g % 2}"].rearrange("p (b k c) -> p b k c", b=2, k=KT) for n in ("whi", "wlo")]
                    for b in range(2):
                        for k in range(KT):
                            if isinstance(j, int) and j == 0 and b == 0:
                                pe.wait_ge(x_lo, 8 * (1 + 2 * f) + k + 1)
                            for i, jj in THREE:
                                ins = t.matmul(bank[g % 2][:, b * T:(b + 1) * T], r32(w[i][:, b, k, :]),
                                               r32((xh, xl)[jj][:, k, :]), start=(k == 0 and i + jj == 0),
                                               stop=(k == KT - 1 and i == 1))
                    ins.then_inc(unit_done, 1)

                def down(j, u, it):
                    pe.wait_ge(d_lo, it * 4 + (FU * f + u + 1))
                    pe.wait_ge(f_lo, it * 4 + (FU * f + u + 1))
                    w = [S[f"{n}{u % 2}"].rearrange("p (n c) -> p n c", n=KT) for n in ("dhi", "dlo")]
                    first = isinstance(j, int) and j == 0
                    last = isinstance(j, int) and j == FU - 1
                    for n in range(KT):
                        for i, jj in THREE:
                            ins = t.matmul(bank[2 + n // 2][:, 256 * (n % 2):256 * (n % 2) + 256],
                                           r32(w[i][:, n, :]), r32(S[f"{('fh', 'fl')[jj]}{u % 2}"]),
                                           start=(first and n % 2 == 0 and i + jj == 0), stop=(last and i == 1),
                                           skip_group_check=True)
                        if last and n % 2:
                            ins.then_inc(bank_full, 1)
                    if not last:
                        ins.then_inc(ffn_used, 1)

                def both(j, u, it):
                    gate_up(j, u, it)
                    down(j - 1, u - 1, it)
                gate_up(0, 0, 0)
                both(1, 1, 0)
                looped(pe, 2, FU, both)
                down(FU - 1, FU - 1, 0)
            swiglu(0)
            norm(5)
            G0 = UNIT0["qkv"]

            def qk_sums(i):
                pe.wait_ge(qk_sq, i + 1)
                if i >= 2:
                    pe.wait_ge(qk_ln, i - 1)
                t.matmul(bank[2 + i % 2][:, :], S["blk"], S["sqh"][:, i % 2, :], start=True, stop=True
                         ).then_inc(qk_sum, 1)
            for j in range(12):
                if j < 8:
                    split_features(G0 + j, xh, xl, 16 if j == 0 else None)
                else:
                    split_rows(G0 + j, xh, xl)
                if j == 0:
                    pe.wait_ge(late_in, 64)
                if 1 <= j <= 8:
                    qk_sums(j - 1)
            pe.wait_ge(qk_ln, 8)
            wait_unit_out(pe, G0 + 10)
            wait_unit_out(pe, G0 + 11)

            def z_scores(h):
                if h == 0:
                    pe.wait_ge(qk_ready, 8)
                if h >= 2:
                    pe.wait_ge(z_ls, h - 1)
                p0, pr = 64 * (h % 2), h // 2
                q, k = S["qT"][p0:p0 + 64, pr, :], S["kT"][p0:p0 + 64, pr, :]
                o = bank[2 + h % 2]
                t.matmul(o[:, 0:T], k[:, 0:P], q, start=True, stop=True)
                t.matmul(o[:, T:T + P], k[:, P:T], q[:, P:T], start=True, stop=True).then_inc(z_ps, 1)

            def z_after(h):
                pe.wait_ge(z_lk, h + 1)
                if h >= 2:
                    pe.wait_ge(z_arg, h - 1)
                o, lk = bank[4 + h % 2], S[f"lk{h % 2}"]
                t.matmul(o[:, 0:T], S["tri"], lk[:, 0:T], start=True, stop=False, skip_group_check=True)
                t.matmul(o[:, P:T], ones[:, :], lk[:, T:T + P], start=False, stop=True, skip_group_check=True)
                t.matmul(o[:, T:T + P], S["tri"], lk[:, T:T + P], start=True, stop=True, skip_group_check=True
                         ).then_inc(z_af, 1)

            def z_value(h):
                pe.wait_ge(z_wm, h + 1)
                pr = h // 2
                if h % 2 == 0 and pr >= 2:
                    pe.wait_ge(z_lo, pr - 1)
                o = bank[6 + pr % 2][64 * (h % 2):64 * (h % 2) + 64, :]
                w = S[f"wz{h % 2}"]
                t.matmul(o[:, 0:T], S["vrow"][:, 0, h * HD:(h + 1) * HD], w[:, 0:T], start=True, stop=False,
                         skip_group_check=True)
                t.matmul(o[:, P:T], S["vrow"][:, 1, h * HD:(h + 1) * HD], w[:, T:T + P], start=False, stop=True,
                         skip_group_check=True).then_inc(z_o, 1)
            for h in range(SBH + 2):
                if h < SBH:
                    z_scores(h)
                if 0 <= h - 1 < SBH:
                    z_after(h - 1)
                if 0 <= h - 2 < SBH:
                    z_value(h - 2)
            pe.wait_ge(z_lo, 8)
            for j in range(4):
                split_features(UNIT0["l1out"] + j, S["oTh"], S["oTl"])
            norm(6)
            swiglu(1)


def tiles(w):
    n = w.shape[1] // 256
    return w.reshape(8, 128, n, 2, 128).transpose(2, 1, 3, 0, 4).reshape(n, 128, 2048)


def ffn_tiles(gate, up, down):
    n = gate.shape[1] // 128
    g, u = (w.reshape(8, 128, n, 128).transpose(2, 1, 0, 3).reshape(n, 128, 1024) for w in (gate, up))
    return np.concatenate([g, u, down.reshape(n, 128, 1024)], axis=2)


def layout(I):
    w = {}
    inp = tiles(I["w_in"][0])
    w["inproj"] = inp[[6, 7, 8, 9, 0, 1, 2, 3, 4, 5, 10, 11, 12, 13]]
    w["outproj"] = tiles(I["w_out"][0])
    w["peerq"] = tiles(I["peer_wq"][0])
    ada = [I[f"l{i}_ada_w_2"].reshape(8, 128, 16, 384).transpose(2, 1, 0, 3).reshape(16, 128, 3072) for i in (0, 1)]
    w["ada"] = np.concatenate(ada, axis=0)
    w["l0in"] = tiles(I["l0_w_in_2"])[[8, 9, 6, 7, 2, 3, 4, 5, 0, 1]]
    w["l0out"] = tiles(I["l0_w_out_2"])
    w["ffn0"] = ffn_tiles(*(I[f"l0_ffn_w_{n}_2"] for n in ("gate", "up", "down")))
    w["qkv"] = tiles(I["l1_w_qkv_2"])
    w["l1out"] = tiles(I["l1_w_out_2"])
    w["ffn1"] = ffn_tiles(*(I[f"l1_ffn_w_{n}_2"] for n in ("gate", "up", "down")))

    def fm(v):
        return v.reshape(-1, 128).T
    c = {"norm1": fm(I["norm1_g"]), "norm2": fm(I["norm2_g"]), "normf": fm(I["normf_g"]),
         "lb": fm(I["rec_lb_logits"]), "recg": fm(I["rec_norm_g"]), "c": fm(I["c_2"]),
         "adab": np.concatenate([fm(I["l0_ada_b_2"]), fm(I["l1_ada_b_2"])], axis=1),
         "mix0": fm(I["l0_mix_norm_2"]), "ffng0": fm(I["l0_ffn_norm_2"]), "mix1": fm(I["l1_mix_norm_2"]),
         "ffng1": fm(I["l1_ffn_norm_2"]), "wa": fm(I["l0_conv_a_w_2"]), "wb": fm(I["l0_conv_b_w_2"]),
         "bb": fm(I["l0_conv_b_b_2"]), "ba": fm(I["l0_rg_a_b_2"]), "bx": fm(I["l0_rg_x_b_2"]),
         "lam": fm(I["l0_rg_lambda_2"]), "qn": np.tile(I["l1_q_norm_2"], 2).reshape(128, 1),
         "kn": np.tile(I["l1_k_norm_2"], 2).reshape(128, 1), "one": np.full((128, 1), 1.0, np.float32),
         "eps": np.full((128, 1), EPS, np.float32)}
    a = {f"w_{k}": v for k, v in w.items()}
    a["xT"] = I["x"][0].T.reshape(8, 128, 256).transpose(1, 0, 2)
    a["cols_d"] = np.concatenate([c[n] for n, _ in COLS], axis=1)
    a["subk_d"] = I["peer_subkeys"][0].reshape(16, 128, 128).transpose(2, 0, 1)
    rg = np.zeros((128, 8, 128), np.float32)
    for i, n in enumerate(("l0_rg_a_w_2", "l0_rg_x_w_2")):
        for h in range(8):
            s = 64 * (h % 2)
            rg[s:s + 64, 4 * i + h // 2, s:s + 64] = I[n][h]
    a["rg_d"] = rg
    a["u_d"], a["v_d"] = I["peer_u"][0], I["peer_v"][0]
    return {k: np.ascontiguousarray(v) for k, v in a.items()}


def constants():
    q, k = np.arange(256)[:, None], np.arange(256)[None, :]
    alibi = np.zeros((128, 6, 512), np.float32)
    for i in range(6):
        for c in range(2 if i < 4 else 4):
            slope = np.float32(2.0 ** (-8.0 * (at_head(i, c) + 1) / HEADS))
            bias = np.where(k <= q, -slope * (q - k).astype(np.float32), np.float32(NEG)).astype(np.float32)
            if i < 4:
                alibi[:, i, 256 * c:256 * c + 256] = bias[128:]
            else:
                alibi[:, i, 128 * c:128 * c + 128] = bias[:128, :128]
    s, t = np.arange(128)[:, None], np.arange(128)[None, :]
    masks = np.stack([((s // b) % 2 == 0) & (t // b == s // b + 1) for b in LEVELS[1:]], axis=1).astype(np.int32)
    before = (s < t).astype(np.float32)
    full = np.ones((128, 128), np.float32)
    sbm = np.stack([np.concatenate([-before, -full, -before], axis=1),
                    np.concatenate([before, full, before], axis=1)], axis=1)
    half = (s // 64 == t // 64).astype(np.float32)
    return {"alibi_d": alibi, "masks_d": masks, "ident_d": np.eye(128, dtype=np.float32),
            "tri_d": (s > t).astype(np.float32), "blk_d": half, "sbmask_d": sbm,
            "iota_d": np.tile(np.arange(16, dtype=np.float32), (128, 1))}


def kernel(**inputs):
    import concourse.bacc as _bacc
    from concourse.bass_utils import run_bass_kernel_spmd as _run

    nc = _bacc.Bacc("TRN2", target_bir_lowering=False, num_devices=1)
    arrays = layout({k: np.asarray(v) for k, v in inputs.items()})
    arrays.update(constants())
    aps = {n: nc.dram_tensor(n, a.shape, mybir.dt.from_np(a.dtype), kind="ExternalInput").ap()
           for n, a in arrays.items()}
    weights = {n[2:]: aps.pop(n) for n in list(aps) if n.startswith("w_")}
    out = nc.dram_tensor("out", (128, 8, 256), F32, kind="ExternalOutput").ap()
    build(nc, w_d=weights, out=out, **aps)
    r = _run(nc, [arrays], core_ids=[0])
    return np.ascontiguousarray(r.results[0]["out"].transpose(1, 0, 2).reshape(1024, 256).T[None])
```
